# Optimizing a Trainium2 kernel written in Bass

```python
import math
import jax, jax.numpy as jnp
from jax import lax
import numpy as np

D_MODEL = 1024
BATCH = 1
SEQ = 512
DEPTH = 1

S5_GROUP = 16
S5_WIDTH = D_MODEL // 2
S5_GROUPS = S5_WIDTH // S5_GROUP
S5_STATE = 64
S5_DT_MIN = 0.001
S5_DT_MAX = 0.1
GLA_HEADS = 4
GLA_VAL_WIDTH = D_MODEL // 2
GLA_DV = GLA_VAL_WIDTH // GLA_HEADS
GLA_DK = GLA_DV // 2
GLA_KEY_WIDTH = GLA_HEADS * GLA_DK
GLA_GATE_RANK = 16
GLA_TAU = 16.0
GLA_CHUNK = 64
D_FF = ((8 * D_MODEL // 3 + 255) // 256) * 256
EPS = 1e-6
IN_SIZES = (S5_WIDTH, GLA_KEY_WIDTH, GLA_KEY_WIDTH, GLA_VAL_WIDTH, GLA_VAL_WIDTH,
            GLA_GATE_RANK, D_MODEL, D_MODEL)
IN_COLS = sum(IN_SIZES)


def rms_norm(x, g):
    xf = x.astype(jnp.float32)
    y = xf * lax.rsqrt(jnp.mean(xf * xf, axis=-1, keepdims=True) + EPS)
    return (y * g.astype(jnp.float32)).astype(x.dtype)

def swiglu(x, w1, w3, w2):
    return (jax.nn.silu(x @ w1) * (x @ w3)) @ w2

def _ssm_combine(e1, e2):
    ar1, ai1, br1, bi1 = e1
    ar2, ai2, br2, bi2 = e2
    return (ar1 * ar2 - ai1 * ai2,
            ar1 * ai2 + ai1 * ar2,
            ar2 * br1 - ai2 * bi1 + br2,
            ar2 * bi1 + ai2 * br1 + bi2)

def s5_mixer(u, lam_re, lam_im, log_dt, b_re, b_im, c_re, c_im, d_skip, w_glu, b_glu):
    bsz, seq, _ = u.shape
    f32 = jnp.float32
    lam_re = lam_re.astype(f32)
    lam_im = lam_im.astype(f32)
    dt = jnp.exp(log_dt.astype(f32))[:, None]
    mag = jnp.exp(lam_re * dt)
    ar = mag * jnp.cos(lam_im * dt)
    ai = mag * jnp.sin(lam_im * dt)
    den = lam_re * lam_re + lam_im * lam_im
    nr = ar - 1.0
    fr = (nr * lam_re + ai * lam_im) / den
    fi = (ai * lam_re - nr * lam_im) / den
    b_re = b_re.astype(f32)
    b_im = b_im.astype(f32)
    bbar_re = fr[:, :, None] * b_re - fi[:, :, None] * b_im
    bbar_im = fr[:, :, None] * b_im + fi[:, :, None] * b_re
    ug = u.astype(f32).reshape(bsz, seq, S5_GROUPS, S5_GROUP)
    bu_re = jnp.einsum('blgh,gph->lbgp', ug, bbar_re)
    bu_im = jnp.einsum('blgh,gph->lbgp', ug, bbar_im)
    a_re = jnp.broadcast_to(ar, (seq, 1, S5_GROUPS, S5_STATE))
    a_im = jnp.broadcast_to(ai, (seq, 1, S5_GROUPS, S5_STATE))
    _, _, xr, xi = lax.associative_scan(_ssm_combine, (a_re, a_im, bu_re, bu_im), axis=0)
    y = (jnp.einsum('ghp,lbgp->blgh', c_re.astype(f32), xr)
         - jnp.einsum('ghp,lbgp->blgh', c_im.astype(f32), xi)
         + d_skip.astype(f32) * ug)
    y = y.reshape(bsz, seq, S5_WIDTH).astype(u.dtype)
    z = jax.nn.gelu(y)
    return z * jax.nn.sigmoid(z @ w_glu + b_glu)

def gla_mixer(q, k, v, r, a_low, w_a_up, b_a_up, g_norm):
    bsz, seq, _ = q.shape
    n_chunks = seq // GLA_CHUNK
    f32 = jnp.float32
    shp_k = (bsz, n_chunks, GLA_CHUNK, GLA_HEADS, GLA_DK)
    shp_v = (bsz, n_chunks, GLA_CHUNK, GLA_HEADS, GLA_DV)
    qc = q.astype(f32).reshape(shp_k) * (GLA_DK ** -0.5)
    kc = k.astype(f32).reshape(shp_k)
    vc = v.astype(f32).reshape(shp_v)
    log_a = jax.nn.log_sigmoid((a_low @ w_a_up + b_a_up).astype(f32)) / GLA_TAU
    bcum = jnp.cumsum(log_a.reshape(shp_k), axis=2)
    b_last = bcum[:, :, -1]
    q_t = qc * jnp.exp(bcum)
    k_t = kc * jnp.exp(-bcum)
    scores = jnp.einsum('bnthd,bnshd->bnhts', q_t, k_t)
    causal = jnp.tril(jnp.ones((GLA_CHUNK, GLA_CHUNK), dtype=bool))
    scores = jnp.where(causal, scores, 0.0)
    o_intra = jnp.einsum('bnhts,bnshv->bnthv', scores, vc)
    k_end = kc * jnp.exp(b_last[:, :, None] - bcum)
    d_state = jnp.einsum('bnshd,bnshv->bnhdv', k_end, vc)
    decay = jnp.exp(b_last)

    def step(state, inp):
        dec, ds = inp
        return dec[..., None] * state + ds, state

    s0 = jnp.zeros((bsz, GLA_HEADS, GLA_DK, GLA_DV), f32)
    _, s_prev = lax.scan(step, s0, (jnp.moveaxis(decay, 1, 0), jnp.moveaxis(d_state, 1, 0)))
    s_prev = jnp.moveaxis(s_prev, 0, 1)
    o_inter = jnp.einsum('bnthd,bnhdv->bnthv', q_t, s_prev)
    o = (o_intra + o_inter).reshape(bsz, seq, GLA_HEADS, GLA_DV)
    o = o * lax.rsqrt(jnp.mean(o * o, axis=-1, keepdims=True) + EPS)
    o = o.reshape(bsz, seq, GLA_VAL_WIDTH) * g_norm.astype(f32)
    return (o * jax.nn.silu(r.astype(f32))).astype(q.dtype)

def first_inputs(seed: int = 0) -> dict:
    key = jax.random.key(seed)
    ks = jax.random.split(key, 32)
    f32 = jnp.float32
    L, G, P, H = DEPTH, S5_GROUPS, S5_STATE, S5_GROUP

    def nrm(k, shape, scale):
        return jax.random.normal(k, shape, f32) * scale

    def gain(k, shape):
        return 1.0 + 0.01 * jax.random.normal(k, shape, f32)

    n_idx = jnp.arange(P, dtype=f32)
    return {
        "x": nrm(ks[0], (BATCH, SEQ, D_MODEL), 1.0),
        "ffn1_norm": gain(ks[1], (L, D_MODEL)),
        "ffn1_w1": nrm(ks[2], (L, D_MODEL, D_FF), D_MODEL ** -0.5),
        "ffn1_w3": nrm(ks[3], (L, D_MODEL, D_FF), D_MODEL ** -0.5),
        "ffn1_w2": nrm(ks[4], (L, D_FF, D_MODEL), D_FF ** -0.5),
        "mix_norm": gain(ks[5], (L, D_MODEL)),
        "w_in": nrm(ks[6], (L, D_MODEL, IN_COLS), D_MODEL ** -0.5),
        "s5_lambda_re": -0.5 + 0.01 * jax.random.normal(ks[7], (L, G, P), f32),
        "s5_lambda_im": math.pi * n_idx + 0.01 * jax.random.normal(ks[8], (L, G, P), f32),
        "s5_log_dt": jax.random.uniform(ks[9], (L, G), f32, math.log(S5_DT_MIN), math.log(S5_DT_MAX)),
        "s5_b_re": nrm(ks[10], (L, G, P, H), (2.0 * H) ** -0.5),
        "s5_b_im": nrm(ks[11], (L, G, P, H), (2.0 * H) ** -0.5),
        "s5_c_re": nrm(ks[12], (L, G, H, P), (2.0 * P) ** -0.5),
        "s5_c_im": nrm(ks[13], (L, G, H, P), (2.0 * P) ** -0.5),
        "s5_d": nrm(ks[14], (L, G, H), 1.0),
        "s5_glu_w": nrm(ks[15], (L, S5_WIDTH, S5_WIDTH), S5_WIDTH ** -0.5),
        "s5_glu_b": nrm(ks[16], (L, S5_WIDTH), 0.01),
        "gla_a_up_w": nrm(ks[17], (L, GLA_GATE_RANK, GLA_KEY_WIDTH), GLA_GATE_RANK ** -0.5),
        "gla_a_up_b": nrm(ks[18], (L, GLA_KEY_WIDTH), 0.1),
        "gla_out_norm": gain(ks[19], (L, GLA_VAL_WIDTH)),
        "proj_s5": nrm(ks[20], (L, S5_WIDTH, D_MODEL), S5_WIDTH ** -0.5),
        "proj_gla": nrm(ks[21], (L, GLA_VAL_WIDTH, D_MODEL), GLA_VAL_WIDTH ** -0.5),
        "w_out": nrm(ks[22], (L, D_MODEL, D_MODEL), D_MODEL ** -0.5),
        "ffn2_norm": gain(ks[23], (L, D_MODEL)),
        "ffn2_w1": nrm(ks[24], (L, D_MODEL, D_FF), D_MODEL ** -0.5),
        "ffn2_w3": nrm(ks[25], (L, D_MODEL, D_FF), D_MODEL ** -0.5),
        "ffn2_w2": nrm(ks[26], (L, D_FF, D_MODEL), D_FF ** -0.5),
        "final_norm": gain(ks[27], (D_MODEL,)),
    }

def first_block(x, ffn1_norm, ffn1_w1, ffn1_w3, ffn1_w2, mix_norm, w_in,
              s5_lambda_re, s5_lambda_im, s5_log_dt, s5_b_re, s5_b_im, s5_c_re, s5_c_im,
              s5_d, s5_glu_w, s5_glu_b, gla_a_up_w, gla_a_up_b, gla_out_norm,
              proj_s5, proj_gla, w_out, ffn2_norm, ffn2_w1, ffn2_w3, ffn2_w2, final_norm):
    split_idx = list(np.cumsum(IN_SIZES)[:-1])
    h = x
    for l in range(DEPTH):
        h = h + 0.5 * swiglu(rms_norm(h, ffn1_norm[l]), ffn1_w1[l], ffn1_w3[l], ffn1_w2[l])
        u = rms_norm(h, mix_norm[l])
        s5_in, q, k, v, r, a_low, g_s5, g_gla = jnp.split(u @ w_in[l], split_idx, axis=-1)
        y_s5 = s5_mixer(s5_in, s5_lambda_re[l], s5_lambda_im[l], s5_log_dt[l],
                        s5_b_re[l], s5_b_im[l], s5_c_re[l], s5_c_im[l], s5_d[l],
                        s5_glu_w[l], s5_glu_b[l])
        y_gla = gla_mixer(q, k, v, r, a_low, gla_a_up_w[l], gla_a_up_b[l], gla_out_norm[l])
        merged = (jax.nn.sigmoid(g_s5) * (y_s5 @ proj_s5[l])
                  + jax.nn.sigmoid(g_gla) * (y_gla @ proj_gla[l]))
        h = h + merged @ w_out[l]
        h = h + 0.5 * swiglu(rms_norm(h, ffn2_norm[l]), ffn2_w1[l], ffn2_w3[l], ffn2_w2[l])
    return rms_norm(h, final_norm).astype(x.dtype)


_first_inputs = first_inputs


def first_inputs(seed=0):
    import zlib

    import numpy as np

    out = dict(_first_inputs(seed))
    spreads = {}
    factors = {'ffn1_norm': 8.0,
     'mix_norm': 8.0,
     's5_lambda_re': 64.0,
     's5_lambda_im': 42.032,
     's5_log_dt': 42.776,
     's5_b_re': 59.728,
     's5_b_im': 59.784,
     's5_c_re': 60.688,
     's5_c_im': 59.12,
     's5_glu_b': 200.0,
     'gla_a_up_b': 4.381,
     'gla_out_norm': 200.0,
     'ffn2_norm': 200.0,
     'final_norm': 200.0,
     's5_d': 3.747,
     's5_glu_w': 5.18,
     'proj_s5': 3.241}
    for name, (base, spread) in spreads.items():
        noise = np.random.default_rng([zlib.crc32(name.encode()), seed]).standard_normal(out[name].shape)
        drawn = base * np.exp(spread * noise) if base else spread * noise
        out[name] = __import__('jax').numpy.asarray(drawn.astype(out[name].dtype))
    for name, factor in factors.items():
        out[name] = (out[name] * factor).astype(out[name].dtype)
    return out


_narrow_inputs = first_inputs


def first_inputs(seed=0):
    out = dict(_narrow_inputs(seed))
    wider = {'s5_glu_b': 12.0, 'gla_out_norm': 4.81, 'ffn2_norm': 4.62, 'final_norm': 7.01}
    for name, times in wider.items():
        mean = out[name].mean()
        out[name] = (mean + times * (out[name] - mean)).astype(out[name].dtype)
    return out


LRU_WIDTH = D_MODEL * 5 // 4
LRU_HEADS = 10
LRU_HEAD_DIM = LRU_WIDTH // LRU_HEADS
LRU_C = 8.0
LRU_CONV = 4
POOL_WIDTH = D_MODEL
POOL_WINDOWS = (2, 4, 8, 16)
POOL_GROUPS = len(POOL_WINDOWS)
POOL_GROUP_DIM = POOL_WIDTH // POOL_GROUPS
N_BRANCHES = 2
IN_WIDTH = LRU_WIDTH + POOL_WIDTH + N_BRANCHES * D_MODEL
D_FF_2 = D_MODEL * 11 // 4
FFN_CONV = 3
RMS_EPS = 1e-6


def rms_norm_2(x, g):
    x32 = x.astype(jnp.float32)
    y = x32 * lax.rsqrt(jnp.mean(x32 * x32, axis=-1, keepdims=True) + RMS_EPS)
    return (y * g.astype(jnp.float32)).astype(x.dtype)

def depthwise_conv(x, w, b, left):
    k_width = w.shape[0]
    s = x.shape[1]
    xp = jnp.pad(x, ((0, 0), (left, k_width - 1 - left), (0, 0)))
    y = b
    for k in range(k_width):
        y = y + w[k] * xp[:, k:k + s]
    return y

def block_diag(x, w, b):
    bsz, s, _ = x.shape
    h, i, j = w.shape
    y = jnp.einsum('bshi,hij->bshj', x.reshape(bsz, s, h, i), w)
    return y.reshape(bsz, s, h * j) + b

def _lin_combine(left, right):
    a_l, b_l = left
    a_r, b_r = right
    return a_l * a_r, a_r * b_l + b_r

def rglru_direction(xc, wa, ba, wx, bx, lam, reverse):
    x32 = xc.astype(jnp.float32)
    r = jax.nn.sigmoid(block_diag(xc, wa, ba).astype(jnp.float32))
    i = jax.nn.sigmoid(block_diag(xc, wx, bx).astype(jnp.float32))
    log_a = -LRU_C * r * jax.nn.softplus(-lam.astype(jnp.float32))
    a = jnp.exp(log_a)
    b_in = jnp.sqrt(-jnp.expm1(2.0 * log_a)) * (i * x32)
    _, h = lax.associative_scan(_lin_combine, (a, b_in), axis=1, reverse=reverse)
    return h

def multiscale_pool(u):
    bsz, s, width = u.shape
    u32 = u.astype(jnp.float32)
    csum = jnp.concatenate([jnp.zeros((bsz, 1, width), jnp.float32),
                            jnp.cumsum(u32, axis=1)], axis=1)
    t = jnp.arange(s)
    outs = []
    for g, w in enumerate(POOL_WINDOWS):
        sl = slice(g * POOL_GROUP_DIM, (g + 1) * POOL_GROUP_DIM)
        cg = csum[..., sl]
        lo = jnp.clip(t - w // 2, 0, s - 1)
        hi = jnp.clip(t + w // 2 - 1, 0, s - 1)
        win_sum = jnp.take(cg, hi + 1, axis=1) - jnp.take(cg, lo, axis=1)
        count = (hi - lo + 1).astype(jnp.float32)[None, :, None]
        outs.append(win_sum / count - u32[..., sl])
    return jnp.concatenate(outs, axis=-1).astype(u.dtype)

def second_inputs(seed: int = 0) -> dict:
    key = jax.random.key(seed)
    ks = jax.random.split(key, 32)
    f32 = jnp.float32
    L = DEPTH

    def nrm(k, shape, scale):
        return jax.random.normal(k, shape, f32) * scale

    def gain(k, shape):
        return 1.0 + 0.05 * jax.random.normal(k, shape, f32)

    def lru_lambda(k):
        u = jax.random.uniform(k, (L, LRU_WIDTH), f32, 0.9, 0.999)
        s = u ** (1.0 / LRU_C)
        return jnp.log(s) - jnp.log1p(-s)

    return {
        "x": jax.random.normal(ks[0], (BATCH, SEQ, D_MODEL), f32),
        "g_mix": gain(ks[1], (L, D_MODEL)),
        "w_in": nrm(ks[2], (L, D_MODEL, IN_WIDTH), D_MODEL ** -0.5),
        "b_gate": nrm(ks[3], (L, N_BRANCHES * D_MODEL), 0.01),
        "conv_a_w": nrm(ks[4], (L, LRU_CONV, LRU_WIDTH), LRU_CONV ** -0.5),
        "conv_a_b": nrm(ks[5], (L, LRU_WIDTH), 0.01),
        "wa_f": nrm(ks[6], (L, LRU_HEADS, LRU_HEAD_DIM, LRU_HEAD_DIM), LRU_HEAD_DIM ** -0.5),
        "ba_f": nrm(ks[7], (L, LRU_WIDTH), 0.01),
        "wx_f": nrm(ks[8], (L, LRU_HEADS, LRU_HEAD_DIM, LRU_HEAD_DIM), LRU_HEAD_DIM ** -0.5),
        "bx_f": nrm(ks[9], (L, LRU_WIDTH), 0.01),
        "lam_f": lru_lambda(ks[10]),
        "wa_b": nrm(ks[11], (L, LRU_HEADS, LRU_HEAD_DIM, LRU_HEAD_DIM), LRU_HEAD_DIM ** -0.5),
        "ba_b": nrm(ks[12], (L, LRU_WIDTH), 0.01),
        "wx_b": nrm(ks[13], (L, LRU_HEADS, LRU_HEAD_DIM, LRU_HEAD_DIM), LRU_HEAD_DIM ** -0.5),
        "bx_b": nrm(ks[14], (L, LRU_WIDTH), 0.01),
        "lam_b": lru_lambda(ks[15]),
        "w_pool": nrm(ks[16], (L, POOL_GROUPS, POOL_GROUP_DIM, POOL_GROUP_DIM), POOL_GROUP_DIM ** -0.5),
        "b_pool": nrm(ks[17], (L, POOL_WIDTH), 0.01),
        "pool_scale": gain(ks[18], (L, POOL_WIDTH)),
        "p_a": nrm(ks[19], (L, LRU_WIDTH, D_MODEL), LRU_WIDTH ** -0.5),
        "p_b": nrm(ks[20], (L, POOL_WIDTH, D_MODEL), POOL_WIDTH ** -0.5),
        "w_out": nrm(ks[21], (L, D_MODEL, D_MODEL), D_MODEL ** -0.5),
        "g_ffn": gain(ks[22], (L, D_MODEL)),
        "w_up": nrm(ks[23], (L, D_MODEL, 2 * D_FF_2), D_MODEL ** -0.5),
        "conv_f_w": nrm(ks[24], (L, FFN_CONV, 2 * D_FF_2), FFN_CONV ** -0.5),
        "conv_f_b": nrm(ks[25], (L, 2 * D_FF_2), 0.01),
        "w_down": nrm(ks[26], (L, D_FF_2, D_MODEL), D_FF_2 ** -0.5),
        "g_final": gain(ks[27], (D_MODEL,)),
    }

def second_block(x, g_mix, w_in, b_gate, conv_a_w, conv_a_b, wa_f, ba_f, wx_f, bx_f, lam_f,
              wa_b, ba_b, wx_b, bx_b, lam_b, w_pool, b_pool, pool_scale, p_a, p_b, w_out,
              g_ffn, w_up, conv_f_w, conv_f_b, w_down, g_final):
    for l in range(DEPTH):
        h = rms_norm_2(x, g_mix[l])
        proj = h @ w_in[l]
        u_a = proj[..., :LRU_WIDTH]
        u_b = proj[..., LRU_WIDTH:LRU_WIDTH + POOL_WIDTH]
        gate_logits = proj[..., LRU_WIDTH + POOL_WIDTH:] + b_gate[l]

        xa = depthwise_conv(u_a, conv_a_w[l], conv_a_b[l], LRU_CONV // 2)
        h_fwd = rglru_direction(xa, wa_f[l], ba_f[l], wx_f[l], bx_f[l], lam_f[l], False)
        h_bwd = rglru_direction(xa, wa_b[l], ba_b[l], wx_b[l], bx_b[l], lam_b[l], True)
        y_a = (h_fwd + h_bwd).astype(x.dtype) @ p_a[l]

        pooled = multiscale_pool(u_b)
        y_b = (block_diag(pooled, w_pool[l], b_pool[l]) * pool_scale[l]) @ p_b[l]

        gates = jax.nn.sigmoid(gate_logits.astype(jnp.float32)).astype(x.dtype)
        merged = gates[..., :D_MODEL] * y_a + gates[..., D_MODEL:] * y_b
        x = x + merged @ w_out[l]

        h = rms_norm_2(x, g_ffn[l])
        up = depthwise_conv(h @ w_up[l], conv_f_w[l], conv_f_b[l], FFN_CONV // 2)
        act = jax.nn.gelu(up[..., :D_FF_2], approximate=True) * up[..., D_FF_2:]
        x = x + act @ w_down[l]
    return rms_norm_2(x, g_final)


def setup_inputs(seed=0):
    out = dict(first_inputs(seed))
    for name, value in second_inputs(seed + 1).items():
        if name != "x":
            out[name + "_2"] = value
    return out


def reference(
    x, ffn1_norm, ffn1_w1, ffn1_w3, ffn1_w2, mix_norm, w_in, s5_lambda_re, s5_lambda_im,
    s5_log_dt, s5_b_re, s5_b_im, s5_c_re, s5_c_im, s5_d, s5_glu_w, s5_glu_b, gla_a_up_w,
    gla_a_up_b, gla_out_norm, proj_s5, proj_gla, w_out, ffn2_norm, ffn2_w1, ffn2_w3, ffn2_w2,
    final_norm, g_mix_2, w_in_2, b_gate_2, conv_a_w_2, conv_a_b_2, wa_f_2, ba_f_2, wx_f_2,
    bx_f_2, lam_f_2, wa_b_2, ba_b_2, wx_b_2, bx_b_2, lam_b_2, w_pool_2, b_pool_2, pool_scale_2,
    p_a_2, p_b_2, w_out_2, g_ffn_2, w_up_2, conv_f_w_2, conv_f_b_2, w_down_2, g_final_2,
):
    x = first_block(
        x, ffn1_norm, ffn1_w1, ffn1_w3, ffn1_w2, mix_norm, w_in, s5_lambda_re, s5_lambda_im,
        s5_log_dt, s5_b_re, s5_b_im, s5_c_re, s5_c_im, s5_d, s5_glu_w, s5_glu_b, gla_a_up_w,
        gla_a_up_b, gla_out_norm, proj_s5, proj_gla, w_out, ffn2_norm, ffn2_w1, ffn2_w3,
        ffn2_w2, final_norm,
    )
    return second_block(
        x, g_mix_2, w_in_2, b_gate_2, conv_a_w_2, conv_a_b_2, wa_f_2, ba_f_2, wx_f_2, bx_f_2,
        lam_f_2, wa_b_2, ba_b_2, wx_b_2, bx_b_2, lam_b_2, w_pool_2, b_pool_2, pool_scale_2,
        p_a_2, p_b_2, w_out_2, g_ffn_2, w_up_2, conv_f_w_2, conv_f_b_2, w_down_2, g_final_2,
    )


_drawn_inputs = setup_inputs


def setup_inputs(seed=0):
    import zlib

    import numpy as np

    out = dict(_drawn_inputs(seed))
    spreads = {}
    factors = {'s5_glu_b': 3.228,
     'g_mix_2': 8.0,
     'w_in_2': 8.0,
     'b_gate_2': 64.0,
     'conv_a_w_2': 64.0,
     'conv_a_b_2': 64.0,
     'wa_f_2': 64.0,
     'ba_f_2': 64.0,
     'wx_f_2': 64.0,
     'bx_f_2': 64.0,
     'lam_f_2': 64.0,
     'wa_b_2': 64.0,
     'ba_b_2': 64.0,
     'wx_b_2': 64.0,
     'bx_b_2': 64.0,
     'lam_b_2': 64.0,
     'w_pool_2': 8.0,
     'b_pool_2': 64.0,
     'pool_scale_2': 8.0,
     'p_a_2': 64.0,
     'p_b_2': 8.0,
     'w_out_2': 8.0,
     'g_ffn_2': 8.0,
     'w_up_2': 8.0,
     'conv_f_w_2': 8.0,
     'conv_f_b_2': 64.0,
     'w_down_2': 8.0}
    for name, (base, spread) in spreads.items():
        noise = np.random.default_rng([zlib.crc32(name.encode()), seed]).standard_normal(out[name].shape)
        drawn = base * np.exp(spread * noise) if base else spread * noise
        out[name] = __import__('jax').numpy.asarray(drawn.astype(out[name].dtype))
    for name, factor in factors.items():
        out[name] = (out[name] * factor).astype(out[name].dtype)
    return out
```

```python
import numpy as np
import concourse.bass as bass
from concourse import mybir
from contextlib import ExitStack

F32 = mybir.dt.float32
F32R = mybir.dt.float32r
U32 = mybir.dt.uint32
ALU = mybir.AluOpType
ACT = mybir.ActivationFunctionType

P = 128
S = 512
D = 1024
KD = D // P
FF = 2816
EPS = 1e-6
HALVES = (12, 10)
assert sum(HALVES) * P == FF
UNIT = 2048

FFN_UNITS = sum(HALVES) + 2 * KD

G5, P5, H5 = 32, 64, 16
T5 = G5 * P5 // P
ROUND = 1.5 * 2.0 ** 23
ROUND13 = 1.5 * 2.0 ** 10
TAU = 2.0 * np.pi
TAU_1 = 6.28125
TAU_2 = float(np.float32(np.round((TAU - TAU_1) * 2.0 ** 21) / 2.0 ** 21))
TAU_3 = float(np.float32(TAU - TAU_1 - TAU_2))

DV, DK, CHUNK = 128, 64, 64
NCH = S // CHUNK
PAIRS = S // P

M1 = {"alow": 0, "k": 1, "q": 2, "v": 3, "r": 5, "s5": 7, "gs": 9, "gg": 13, "pgla": 17, "glu": 21,
      "ps5": 23, "wout": 27}
M1_UNITS = 31

HEADS = 10
LRU_C = 8.0
WINDOWS = (2, 4, 8, 16)
EDGE = max(WINDOWS) // 2

M2 = {"ua": (0, 1, 2, 3, 4), "ub": (5, 6, 8, 10), "wp": (7, 9, 11, 13), "gb": (12, 14, 15, 16),
      "pb": (17, 18, 19, 20), "ga": (21, 22, 23, 24), "pa": tuple(range(25, 33)), "wout": (33, 34, 35, 36)}
M2_UNITS = 37
M2_KIND = {i: (name, u) for name, at in M2.items() for u, i in enumerate(at)}
LRU_AT = M2["wp"][-1] + 1


class Tally:

    def __init__(self, sem):
        self.sem, self.base, self.local, self.turn, self.per = sem, 0, 0, None, 0

    def step(self, by=1):
        self.local += by
        return self.value()

    def value(self):
        if self.turn is None:
            return self.base + self.local
        return (self.turn - 1) * self.per + (self.base + self.local)


def rolled(eng, turns, body, tallies):
    before = [t.base + t.local for t in tallies]
    body(0)
    for t, b in zip(tallies, before):
        t.base, t.local = t.base + t.local, 0
        t.per = t.base - b
    with eng.Fori(1, turns) as it:
        for t in tallies:
            t.turn = it
        body(it)
    for t in tallies:
        assert t.local == t.per
        t.base, t.local, t.turn = t.base + (turns - 1) * t.per, 0, None


def rolled_on(eng, start, end, body, tallies):
    before = [t.base + t.local for t in tallies]
    body(start)
    for t, b in zip(tallies, before):
        t.base, t.local = t.base + t.local, 0
        t.per = t.base - b
    with eng.Fori(start + 1, end) as it:
        for t in tallies:
            t.turn = it - start
        body(it)
    for t in tallies:
        assert t.local == t.per
        t.base, t.local, t.turn = t.base + (end - start - 1) * t.per, 0, None


def columns(names_widths):
    at, out = 0, {}
    for name, width in names_widths:
        out[name] = at
        at += width
    return out, at


VECS, N_VECS = columns([("ffn1_norm", 8), ("mix_norm", 8), ("ffn2_norm", 8), ("final_norm", 8),
                        ("g_mix_2", 8), ("g_ffn_2", 8), ("g_final_2", 8),
                        ("gla_a_up_b", 2), ("gla_out_norm", 4), ("s5_d", 4), ("s5_glu_b", 4),
                        ("lam_re", 16), ("lam_im", 16), ("log_dt", 16),
                        ("b_gate_2", 16), ("conv_a_w_2", 40), ("conv_a_b_2", 10),
                        ("ba_f_2", 10), ("bx_f_2", 10),
                        ("ba_b_2", 10), ("bx_b_2", 10), ("lam_f_2", 10), ("lam_b_2", 10),
                        ("b_pool_2", 8), ("pool_scale_2", 8),
                        ("conv_f_w_2", 132), ("conv_f_b_2", 44)])


def build(nc, A, out):
    ctx = ExitStack()
    with ctx:
        def sem(name):
            return ctx.enter_context(nc.semaphore(name))

        top = [16512]

        def put(name, shape, dt=F32, at=None):
            size = 4 * int(np.prod(shape[1:]))
            if at is None:
                at, top[0] = top[0], top[0] + -(-size // 32) * 32
            t = nc.alloc_sbuf_tensor_at(name, shape, dt, offset=at)
            return t

        vec = put("vec", [P, N_VECS])
        ident = put("ident", [P, P])
        ones = put("ones", [P, P])
        acc = put("acc", [P, S])
        sq = put("sq", [P, S])
        diag = put("diag", [P, 4, P])
        ut = put("ut", [P, 2, S])
        nstat = put("nstat", [P, 16])
        aup = put("aup", [P, 2 * P])
        causal = put("causal", [P, P])
        raw = [put(f"raw{i}", [P, UNIT]) for i in range(2)]
        whi = [put(f"whi{i}", [P, UNIT], F32R) for i in range(2)]
        wlo = [put(f"wlo{i}", [P, UNIT], F32R) for i in range(2)]
        v5 = put("v5", [P, 14, T5])
        lam = put("lam", [P, 5, 2 * HEADS])
        per_count = put("per_count", [P, len(WINDOWS), 2 * EDGE])
        uhi = put("uhi", [P, KD, S], F32R)
        ulo = put("ulo", [P, KD, S], F32R)
        region = top[0]
        x = put("x", [P, KD, S])
        hhi = put("hhi", [P, max(HALVES), S], F32R)
        hlo = put("hlo", [P, max(HALVES), S], F32R)
        sil = put("sil", [P, 2, S])
        ht = put("ht", [P, 2, S])
        cva = put("cva", [P, 2, S])
        cvb = put("cvb", [P, 2, S])

        steps5 = put("steps5", [P, S])
        turn_t = put("turn_t", [P, 2, S])
        turn = put("turn", [P, 2, S])
        turn_c = put("turn_c", [P, 2, S])
        turn_s = put("turn_s", [P, 2, S])
        turn_q = put("turn_q", [P, 2, S])
        trig = put("trig", [P, 2, 2 * S])
        assert top[0] <= 229344

        def at_kb(kb):
            return region + int(kb * 1024)

        trig5 = put("trig5", [P, 2, 2 * S], at=at_kb(0))
        bc5 = put("bc5", [P, 2, 4 * P], at=at_kb(8))
        c5 = put("c5", [P, 2, 2 * P], at=at_kb(12))
        s5in = put("s5in", [P, 4, S], at=at_kb(16))
        rot = put("rot", [P, 2, 2, S], at=at_kb(24))
        state5 = put("state5", [P, 2, 2, S], at=at_kb(32))
        ys_hi = put("ys_hi", [P, 4, S], F32R, at=at_kb(24))
        ys_lo = put("ys_lo", [P, 4, S], F32R, at=at_kb(32))
        yg_hi = put("yg_hi", [P, 4, S], F32R, at=at_kb(40))
        yg_lo = put("yg_lo", [P, 4, S], F32R, at=at_kb(48))
        eq = put("eq", [P, 2, S], at=at_kb(56))
        lt = put("lt", [P, 2, S], at=at_kb(60))
        alow = put("alow", [P, S], at=at_kb(64))
        s_t = put("s_t", [P, 2, 4, P], at=at_kb(66))
        la = put("la", [P, 2, S], at=at_kb(70))
        kend_t = put("kend_t", [P, PAIRS, 2, P], at=at_kb(70))
        ek = put("ek", [P, 2, S], at=at_kb(74))
        q_f = put("q_f", [P, 2, S], at=at_kb(78))
        k_f = put("k_f", [P, 2, S], at=at_kb(82))
        v_t = put("v_t", [P, PAIRS, 4 * DV], at=at_kb(86))
        r_f = put("r_f", [P, 4, S], at=at_kb(94))
        first_of_chunk = put("first_of_chunk", [P, S], at=at_kb(102))
        st = put("st", [P, 2, NCH + 1, DV], at=at_kb(102))
        decay = put("decay", [P, 2, NCH], at=at_kb(111))
        gate = put("gate", [P, 16, S], at=at_kb(56))
        z_f = put("z_f", [P, 4, S], at=at_kb(88))
        z_hi = put("z_hi", [P, 4, S], F32R, at=at_kb(96))
        z_lo = put("z_lo", [P, 4, S], F32R, at=at_kb(104))

        xa = put("xa", [P, HEADS, S], at=at_kb(0))
        ya_hi = put("ya_hi", [P, HEADS, S], F32R, at=at_kb(0))
        ya_lo = put("ya_lo", [P, HEADS, S], F32R, at=at_kb(20))
        lru_i = put("lru_i", [P, 2, 2, S], at=at_kb(38))
        lru_a = put("lru_a", [P, 2, 2, S], at=at_kb(46))
        lru_v = put("lru_v", [P, 2, 2, S], at=at_kb(54))
        pool_hi = put("pool_hi", [P, 2, 2, S], F32R, at=at_kb(38))
        pool_lo = put("pool_lo", [P, 2, 2, S], F32R, at=at_kb(46))
        win = [put(f"win{i}", [P, S + 2 * EDGE], at=at_kb(54) + 2112 * i) for i in range(3)]
        wg = [diag, put("wg1", [P, 4, P], at=at_kb(62))]
        t_hi = put("t_hi", [P, KD, S], F32R, at=at_kb(64))
        t_lo = put("t_lo", [P, KD, S], F32R, at=at_kb(80))
        gate_a = put("gate_a", [P, KD, S], at=at_kb(64))
        gate_b = put("gate_b", [P, KD, S], at=at_kb(96))
        assert at_kb(112) <= 229344, at_kb(112)

        x_kept = nc.dram_tensor("x_kept", [KD, P, S], F32, kind="Internal").ap()
        trig_kept = nc.dram_tensor("trig_kept", [T5, P, 2 * S], F32, kind="Internal").ap()

        bank = [ctx.enter_context(nc.psum_tensor(f"bank{i}", [P, S], F32)) for i in range(8)]
        DB = [bank[0:2], bank[2:4]]
        XB = bank[4:8]

        vec_in = sem("vec_in")
        x_in = sem("x_in")
        const_made = sem("const_made")
        raw_landed = [sem("raw_landed0"), sem("raw_landed1")]
        w_hi = sem("w_hi")
        w_lo = sem("w_lo")
        pe_done = sem("pe_done")
        evac = [sem("evac0"), sem("evac1")]
        act_tile = sem("act_tile")
        conv_done = sem("conv_done")
        h_ready = sem("h_ready")
        acc_ready = sem("acc_ready")
        sums_out = sem("sums_out")
        rt_ready = sem("rt_ready")
        rs_ready = sem("rs_ready")
        diag_ready = sem("diag_ready")
        spread = sem("spread")
        ut_ready = sem("ut_ready")
        uhi_ready = sem("uhi_ready")
        u_ready = sem("u_ready")
        dve_step = sem("dve_step")
        pool_step = sem("pool_step")
        act_step = sem("act_step")
        stored = sem("stored")
        out_ready = sem("out_ready")
        s5_exp = sem("s5_exp")
        s5_angle = sem("s5_angle")
        s5_vecs = sem("s5_vecs")
        turned = sem("turned")
        sines = sem("sines")
        trig_ready = sem("trig_ready")
        trig_out = [sem("trig_out0"), sem("trig_out1")]
        x_done = sem("x_done")
        spilled = sem("spilled")
        x_back = sem("x_back")
        aup_in = sem("aup_in")
        aup_out = sem("aup_out")
        z_neg = sem("z_neg")
        ln_out = sem("ln_out")
        bcum = sem("bcum")
        exps_out = sem("exps_out")
        rest_ready = sem("rest_ready")
        rest_exp = sem("rest_exp")
        gla_in = sem("gla_in")
        kend_out = sem("kend_out")
        kend_in = sem("kend_in")
        scores_out = sem("scores_out")
        masked = sem("masked")
        dstate_out = sem("dstate_out")
        state_in = sem("state_in")
        o_out = sem("o_out")
        o_kept = sem("o_kept")
        yg_ready = sem("yg_ready")
        r_ready = sem("r_ready")
        gate_ready = sem("gate_ready")
        side5_in = [sem("side5_in0"), sem("side5_in1")]
        bu_out = sem("bu_out")
        bu_read = sem("bu_read")
        scanned = sem("scanned")
        c5_ready = sem("c5_ready")
        re_ready = sem("re_ready")
        im_ready = sem("im_ready")
        y5_out = sem("y5_out")
        z_sum = sem("z_sum")
        z_act = sem("z_act")
        z_ready = sem("z_ready")
        glu_act = sem("glu_act")
        glu_used = sem("glu_used")
        ys_ready = sem("ys_ready")
        lam_exp = sem("lam_exp")
        wg_in = [sem("wg_in0"), sem("wg_in1")]
        xa_ready = sem("xa_ready")
        pooled = sem("pooled")
        t_ready = sem("t_ready")
        lru_out = sem("lru_out")
        lru_gates = sem("lru_gates")
        lru_exp = sem("lru_exp")
        lru_var = sem("lru_var")
        lru_root = sem("lru_root")
        ya_ready = sem("ya_ready")
        gate2_ready = sem("gate2_ready")

        BASES = {"ffn1": 0}

        def slot5(j):
            at = 7 * j // 2
            return M1["gs"] + 1 + at // KD, at % KD

        block = ctx.enter_context(nc.Block())

        @block.sync
        def _(sp):
            def load(nb, it, src, width):
                if not (isinstance(it, int) and nb + 2 * it < 2):
                    sp.wait_ge(w_lo, nb - 1 + 2 * it)
                sp.dma_start(raw[nb % 2][:, 0:width], src).then_inc(raw_landed[nb % 2], 16)

            def ffn(nb, up, down, side=None):
                m0 = 0
                for h, tiles in enumerate(HALVES):
                    def up_turn(it):
                        for j in range(2):
                            load(nb + j, it, up[m0 + j + 2 * it], UNIT)

                    def down_turn(it):
                        for j in range(2):
                            load(nb + j, it, down[h][j + 2 * it], tiles * P)
                        if side:
                            side(h, it)
                    rolled(sp, tiles // 2, up_turn, [])
                    nb += tiles
                    rolled(sp, KD // 2, down_turn, [])
                    nb += KD
                    m0 += tiles

            def mixer1(nb):
                src = [A["win1_alow"][0]] + [A["win1"][i] for i in range(16)] \
                    + [A["pgla"][i] for i in range(4)] + [A["glu"][i] for i in range(2)] \
                    + [A["ps5"][i] for i in range(4)] + [A["wout1"][i] for i in range(4)]
                assert len(src) == M1_UNITS

                def side5(j):
                    if j == 0:
                        sp.wait_ge(spilled, 16 * KD)
                        for q in range(2):
                            sp.wait_ge(trig_out[q], 16 * T5 // 2)
                    if j >= 2:
                        sp.wait_ge(re_ready, j - 1)
                        sp.wait_ge(im_ready, j - 1)
                    sp.dma_start(trig5[:, j % 2, :], trig_kept[j]).then_inc(side5_in[j % 2], 16)
                    sp.dma_start(bc5[:, j % 2, :], A["bc5"][j]).then_inc(side5_in[j % 2], 16)

                sent = 0
                for i in range(M1_UNITS):
                    load(nb + i, 0, src[i], src[i].shape[-1])
                    if i == 0:
                        for k in range(KD):
                            if k == 0:
                                sp.wait_ge(x_done, 1)
                            sp.dma_start(x_kept[k], x[:, k, :]).then_inc(spilled, 16)
                    while sent < T5 and i >= M1["gs"] + 1 and (sent < 2 or slot5(sent)[0] <= i - 1):
                        side5(sent)
                        sent += 1
                    if i == M1["wout"] - 1:
                        sp.wait_ge(y5_out, T5)
                        sp.wait_ge(c5_ready, T5)
                        for k in range(KD):
                            sp.dma_start(x[:, k, :], x_kept[k]).then_inc(x_back, 16)
                assert sent == T5

            def mixer2(nb):
                for i in range(M2_UNITS):
                    name, u = M2_KIND[i]
                    src = A[name + "2"][u]
                    load(nb + i, 0, src, src.shape[-1])
                    if i == 0:
                        sp.wait_ge(x_done, 2)
                        for k in range(KD):
                            sp.dma_start(x_kept[k], x[:, k, :]).then_inc(spilled, 16)
                    h = i - LRU_AT + 1
                    if 0 <= h < HEADS:
                        if h == 0:
                            sp.wait_ge(spilled, 2 * 16 * KD)
                        if h >= 2:
                            sp.wait_ge(lru_out, h - 1)
                        sp.dma_start(wg[h % 2][:, :, :], A["wg2"][h]).then_inc(wg_in[h % 2], 16)
                    if i == M2["wout"][1]:
                        sp.wait_ge(pe_done, nb + M2["pa"][-1] + 1)
                        for k in range(KD):
                            sp.dma_start(x[:, k, :], x_kept[k]).then_inc(x_back, 16)

            for k in range(KD):
                sp.dma_start(x[:, k, :], A["xT"][k * P:(k + 1) * P, :]).then_inc(x_in, 16)
            sp.dma_start(vec[:, :], A["vec"]).then_inc(vec_in, 16)
            sp.dma_start(aup[:, :], A["aup"]).then_inc(aup_in, 16)

            def keep_trig(h, it):
                for j in range(2):
                    sp.wait_ge(trig_ready, KD * h + 2 * it + j + 1)
                    sp.dma_start(trig_kept[KD * h + j + 2 * it], trig[:, j, :]).then_inc(trig_out[j], 16)

            ffn(0, A["up1"], (A["down1a"], A["down1b"]), keep_trig)
            mixer1(FFN_UNITS)
            nb = FFN_UNITS + M1_UNITS
            ffn(nb, A["up2"], (A["down2a"], A["down2b"]))
            mixer2(nb + FFN_UNITS)
            nb += FFN_UNITS + M2_UNITS
            ffn(nb, A["up3"], (A["down3a"], A["down3b"]))
            for k in range(KD):
                sp.wait_ge(out_ready, k + 1)
                sp.dma_start(out[k * P:(k + 1) * P, :], x[:, k, :]).then_inc(stored, 16)
            sp.wait_ge(stored, 16 * KD)

        @block.gpsimd
        def _(pool):
            def low(nb, it, width):
                pool.wait_ge(w_hi, nb + 1 + 2 * it)
                s = nb % 2
                pool.tensor_tensor(out=wlo[s][:, 0:width], in0=raw[s][:, 0:width],
                                   in1=whi[s][:, 0:width].bitcast(F32), op=ALU.subtract).then_inc(w_lo, 1)

            steps = Tally(pool_step)

            def then(ins):
                ins.then_inc(pool_step, 1)
                pool.wait_ge(pool_step, steps.step())

            norms = Tally(rt_ready)

            def inverse_root():
                pool.wait_ge(rt_ready, norms.step())
                pool.tensor_tensor(out=nstat[:, 4:8], in0=nstat[:, 0:4], in1=nstat[:, 8:12],
                                   op=ALU.pow).then_inc(rs_ready, 1)

            def ffn(nb, first=None):
                for h, tiles in enumerate(HALVES):
                    def up_turn(it):
                        for j in range(2):
                            low(nb + j, it, UNIT)
                            if h == 0 and j == 0 and isinstance(it, int) and first:
                                first()

                    def down_turn(it):
                        for j in range(2):
                            low(nb + j, it, tiles * P)
                    rolled(pool, tiles // 2, up_turn, [])
                    nb += tiles
                    rolled(pool, KD // 2, down_turn, [])
                    nb += KD

            def mixer1(nb):
                widths = [D] + 16 * [UNIT] + 10 * [4 * 2 * P] + 4 * [UNIT]

                def imaginary(j):
                    q = j % 2
                    pool.wait_ge(side5_in[q], 32 * (j // 2 + 1))
                    pool.wait_ge(scanned, 2 * (j + 1))
                    pool.tensor_tensor(out=ut[:, 0, :], in0=rot[:, q, 0, :], in1=trig5[:, q, S:2 * S], op=ALU.mult)
                    then(pool.tensor_tensor(out=ut[:, 1, :], in0=rot[:, q, 1, :], in1=trig5[:, q, 0:S], op=ALU.mult))
                    if j >= 2:
                        pool.wait_ge(y5_out, j - 1)
                    pool.tensor_tensor(out=state5[:, q, 1, :], in0=ut[:, 0, :], in1=ut[:, 1, :], op=ALU.add)\
                        .then_inc(im_ready, 1)
                    pool.wait_ge(im_ready, j + 1)

                done5 = 0
                for i in range(M1_UNITS):
                    low(nb + i, 0, widths[i])
                    if i == 0:
                        inverse_root()
                    if M1["r"] + 1 <= i < M1["r"] + 1 + PAIRS:
                        inverse_root()
                    while done5 < T5 and slot5(done5)[0] <= i - 1:
                        if done5 == 0:
                            pool.wait_ge(yg_ready, PAIRS)
                        imaginary(done5)
                        done5 += 1
                assert done5 == T5

            pool.iota(steps5[:, :], pattern=[[1, S]], base=0, channel_multiplier=0,
                      allow_small_or_imprecise_dtypes=True)
            pool.memset(nstat[:, 12:13], float(np.pi / 2))
            for n, w in enumerate(WINDOWS):
                last = pool.memset(per_count[:, n, :], 1.0 / w)
            then(last)
            for n, w in enumerate(WINDOWS):
                for e in range(w // 2):
                    pool.memset(per_count[:, n, e:e + 1], 1.0 / (e + w // 2))
                for e in range(1, w // 2):
                    pool.memset(per_count[:, n, 2 * EDGE - e:2 * EDGE - e + 1], 1.0 / (e + w // 2))
            then(pool.memset(causal[:, :], 1.0))
            then(pool.affine_select(out=causal[:, :], in_=causal[:, :], compare_op=ALU.is_ge, fill=0.0, base=0,
                                    pattern=[[1, P]], channel_multiplier=-1))
            pool.memset(causal[0:CHUNK, CHUNK:P], 0.0)
            pool.memset(ones[:, :], 1.0)
            pool.memset(nstat[:, 8:12], -0.5)
            then(pool.memset(ident[:, :], 0.0))
            pool.affine_select(out=ident[:, :], in_=ident[:, :], compare_op=ALU.not_equal, fill=1.0, base=0,
                               pattern=[[-1, P]], channel_multiplier=1).then_inc(const_made, 1)
            pool.wait_ge(const_made, 1)
            ffn(0, inverse_root)
            mixer1(FFN_UNITS)
            nb = FFN_UNITS + M1_UNITS
            ffn(nb, inverse_root)
            nb += FFN_UNITS
            for i in range(M2_UNITS):
                low(nb + i, 0, A[M2_KIND[i][0] + "2"].shape[-1])
                if i == 0:
                    inverse_root()
                    inverse_root()
            nb += M2_UNITS
            ffn(nb, inverse_root)
            inverse_root()

        @block.scalar
        def _(act):
            def high(nb, it, width):
                s = nb % 2
                act.wait_ge(raw_landed[s], 16 * (nb // 2 + 1) + 16 * it)
                if not (isinstance(it, int) and nb + 2 * it < 2):
                    act.wait_ge(pe_done, nb - 1 + 2 * it)
                act.activation(whi[s][:, 0:width], raw[s][:, 0:width], ACT.Copy).then_inc(w_hi, 1)

            steps = Tally(act_step)
            turns = Tally(turned)

            def then(ins):
                ins.then_inc(act_step, 1)
                act.wait_ge(act_step, steps.step())

            half_pi = nstat[:, 12:13]

            def small5():
                lams = vec[:, VECS["lam_f_2"]:VECS["lam_f_2"] + 2 * HEADS]
                then(act.activation(lam[:, 2, :], lams, ACT.Abs))
                act.activation(lam[:, 2, :], lam[:, 2, :], ACT.Exp, scale=-1.0).then_inc(lam_exp, 1)
                act.activation(v5[:, 0, :], vec[:, VECS["log_dt"]:VECS["log_dt"] + T5], ACT.Exp).then_inc(s5_exp, 1)
                act.wait_ge(s5_angle, 1)
                act.activation(v5[:, 1, :], v5[:, 1, :], ACT.Exp)
                then(act.activation(v5[:, 4, :], v5[:, 3, :], ACT.Abs))
                act.activation(v5[:, 5, :], v5[:, 3, :], ACT.Sin, scale=0.5)
                act.activation(v5[:, 6, :], v5[:, 4, :], ACT.Sin, scale=-0.5, bias=half_pi).then_inc(s5_exp, 1)

            def trig_tiles():
                for j in range(2):
                    act.wait_ge(turned, turns.step())
                    act.activation(turn_s[:, j, :], turn[:, j, :], ACT.Sin, scale=float(np.pi))
                    then(act.activation(turn_c[:, j, :], turn[:, j, :], ACT.Abs))
                    act.activation(turn_c[:, j, :], turn_c[:, j, :], ACT.Sin, scale=-float(np.pi), bias=half_pi)
                    act.activation(turn_q[:, j, :], turn_s[:, j, :], ACT.Square, scale=float(np.sqrt(2.0)))\
                        .then_inc(sines, 1)

            def mixer1(nb):
                widths = [D] + 16 * [UNIT] + 10 * [4 * 2 * P] + 4 * [UNIT]

                def bank_of(i, m):
                    return DB[(nb + i) % 2][m][:, :]

                def log_gate():
                    for m in range(2):
                        act.wait_ge(z_neg, m + 1)
                        b = VECS["gla_a_up_b"] + m
                        last = act.activation(lt[:, m, :], XB[m][:, :], ACT.Abs, bias=vec[:, b:b + 1])
                    then(last)
                    then(act.activation(lt[:, :, :], lt[:, :, :], ACT.Exp, scale=-1.0))
                    act.activation(lt[:, :, :], lt[:, :, :], ACT.Ln, bias=ones[:, 0:1]).then_inc(ln_out, 1)

                def decays():
                    act.wait_ge(bcum, 2)
                    act.activation(eq[:, :, :], la[:, :, :], ACT.Exp, scale=1.0 / 16)
                    act.activation(ek[:, :, :], la[:, :, :], ACT.Exp, scale=-1.0 / 16).then_inc(exps_out, 1)

                def decay_rest():
                    act.wait_ge(rest_ready, 1)
                    act.activation(lt[:, :, :], lt[:, :, :], ACT.Exp, scale=1.0 / 16).then_inc(rest_exp, 1)

                def keep_kend():
                    act.wait_ge(kend_out, 1)
                    for half in range(2):
                        act.activation(kend_t[:, 2 * half:2 * half + 2, :, :], XB[half][:, :], ACT.Copy)\
                            .then_inc(kend_in, 1)

                def keep_o(p):
                    act.wait_ge(o_out, p + 1)
                    if p:
                        act.wait_ge(yg_ready, p)
                    act.activation(ut[:, 0, :], XB[3][:, :], ACT.Copy)
                    act.activation(ut[:, 1, :], XB[3][:, :], ACT.Square).then_inc(o_kept, 1)

                def silu_r(u):
                    i = M1["r"] + u
                    act.wait_ge(pe_done, nb + i + 1)
                    act.activation(r_f[:, 2 * u, :], bank_of(i, 0), ACT.Silu).then_inc(r_ready, 1)
                    act.activation(r_f[:, 2 * u + 1, :], bank_of(i, 1), ACT.Silu).then_inc(evac[(nb + i) % 2], 1)
                    act.wait_ge(evac[(nb + i) % 2], (nb + i) // 2 + 1)
                    act.nop().then_inc(r_ready, 1)

                def sigmoids(u):
                    i = M1["gs"] + u
                    act.wait_ge(pe_done, nb + i + 1)
                    if u == 1:
                        act.wait_ge(yg_ready, PAIRS)
                    act.activation(gate[:, 2 * u, :], bank_of(i, 0), ACT.Sigmoid).then_inc(gate_ready, 1)
                    act.activation(gate[:, 2 * u + 1, :], bank_of(i, 1), ACT.Sigmoid).then_inc(evac[(nb + i) % 2], 1)

                def gelu_z(m):
                    act.wait_ge(z_sum, m + 1)
                    act.activation(z_f[:, m, :], z_f[:, m, :], ACT.Gelu_apprx_tanh).then_inc(z_act, 1)

                def glu(u):
                    i = M1["glu"] + u
                    act.wait_ge(pe_done, nb + i + 1)
                    for m in range(2):
                        if u:
                            act.wait_ge(glu_used, m + 1)
                        b = VECS["s5_glu_b"] + 2 * u + m
                        a = act.activation(ut[:, m, :], bank_of(i, m), ACT.Sigmoid, bias=vec[:, b:b + 1])
                        a.then_inc(glu_act, 1)

                jobs = {1: [norm_high], 2: [log_gate], 3: [decays], 4: [decay_rest],
                        6: [keep_kend, lambda: silu_r(0)], 7: [lambda: keep_o(0), lambda: silu_r(1)],
                        8: [lambda: keep_o(1)], 9: [lambda: keep_o(2)], 10: [lambda: keep_o(3)]}
                for u in range(8):
                    jobs.setdefault(M1["gs"] + u + 1, []).append(lambda u=u: sigmoids(u))
                for m, i in enumerate((13, 15, 17, 20)):
                    jobs.setdefault(i, []).insert(0, lambda m=m: gelu_z(m))
                for u in range(2):
                    jobs.setdefault(M1["glu"] + u + 1, []).append(lambda u=u: glu(u))
                for i in range(M1_UNITS):
                    high(nb + i, 0, widths[i])
                    for job in jobs.get(i, ()):
                        job()

            def mixer2(nb):
                def bank_of(i, m):
                    return DB[(nb + i) % 2][m][:, :]

                def gates(name, u):
                    i = M2[name][u]
                    dst, b = (gate_a, 0) if name == "ga" else (gate_b, 8)
                    act.wait_ge(pe_done, nb + i + 1)
                    for m in range(2):
                        c = VECS["b_gate_2"] + b + 2 * u + m
                        last = act.activation(dst[:, 2 * u + m, :], bank_of(i, m), ACT.Sigmoid, bias=vec[:, c:c + 1])
                    last.then_inc(evac[(nb + i) % 2], 1)

                def lru_functions(h):
                    q = h % 2
                    if h >= 2:
                        act.wait_ge(ya_ready, h - 1)
                    if h:
                        act.wait_ge(lru_exp, 2 * h)
                    act.wait_ge(lru_out, h + 1)
                    for d in range(2):
                        for n, (name, dst) in enumerate((("ba", ut[:, d, :]), ("bx", lru_i[:, q, d, :]))):
                            c = VECS[name + "_" + "fb"[d] + "_2"] + h
                            last = act.activation(dst, XB[2 * d + n][:, :], ACT.Sigmoid, bias=vec[:, c:c + 1])
                    last.then_inc(lru_gates, 1)
                    act.wait_ge(lru_gates, h + 1)
                    for d in range(2):
                        c = d * HEADS + h
                        act.activation(lru_v[:, q, d, :], ut[:, d, :], ACT.Tanh, scale=lam[:, 0, c:c + 1])
                    for d in range(2):
                        c = d * HEADS + h
                        act.activation(lru_a[:, q, d, :], ut[:, d, :], ACT.Exp, scale=lam[:, 1, c:c + 1])\
                            .then_inc(lru_exp, 1)

                def lru_roots(h):
                    q = h % 2
                    act.wait_ge(lru_var, 2 * (h + 1))
                    for d in range(2):
                        act.activation(lru_v[:, q, d, :], lru_v[:, q, d, :], ACT.Sqrt).then_inc(lru_root, 1)

                for i in range(M2_UNITS):
                    high(nb + i, 0, A[M2_KIND[i][0] + "2"].shape[-1])
                    if i == 1:
                        norm_high()
                    h = i - 1 - LRU_AT
                    if 0 <= h < HEADS:
                        lru_functions(h)
                        if h:
                            lru_roots(h - 1)
                        if h == HEADS - 1:
                            lru_roots(h)
                    if i and M2_KIND[i - 1][0] in ("ga", "gb"):
                        gates(*M2_KIND[i - 1])

            tiles_u = Tally(ut_ready)

            def norm_high():
                for k in range(KD):
                    act.wait_ge(ut_ready, tiles_u.step())
                    act.activation(uhi[:, k, :], ut[:, k % 2, :], ACT.Copy).then_inc(uhi_ready, 1)

            convs = Tally(conv_done)

            def gate_tile(nb, it, func):
                s = nb % 2
                if func == ACT.Silu:
                    act.wait_ge(pe_done, nb + 1 + 2 * it)
                    act.activation(sil[:, s, :], DB[s][0][:, :], ACT.Silu).then_inc(act_tile, 1)
                else:
                    act.wait_ge(conv_done, convs.step())
                    act.activation(sil[:, s, :], cva[:, s, :], ACT.Gelu_apprx_tanh).then_inc(act_tile, 1)

            def ffn(nb, func, first=None, side=None):
                for h, tiles in enumerate(HALVES):
                    def up_turn(it):
                        alone = isinstance(it, int)
                        for j in range(2):
                            high(nb + j, it, UNIT)
                            if not alone:
                                gate_tile(nb + j, it - 1, func)
                        if alone and h == 0 and first:
                            first()

                    def down_turn(it):
                        for j in range(2):
                            high(nb + j, it, tiles * P)
                            if isinstance(it, int):
                                gate_tile(nb - 2 + j, 0, func)
                        if side:
                            side()
                    up_turn(0)
                    with act.Fori(1, tiles // 2) as it:
                        convs.base, convs.local, convs.per, convs.turn = convs.base + convs.local, 0, 2, it
                        up_turn(it)
                    if func == ACT.Gelu_apprx_tanh:
                        convs.base += 2 * (tiles // 2 - 1)
                    convs.local, convs.turn = 0, None
                    nb += tiles
                    rolled(act, KD // 2, down_turn, [turns, steps])
                    nb += KD

            act.wait_ge(vec_in, 16)
            act.wait_ge(const_made, 1)

            def first():
                norm_high()
                small5()
            ffn(0, ACT.Silu, first, trig_tiles)
            mixer1(FFN_UNITS)
            nb = FFN_UNITS + M1_UNITS
            ffn(nb, ACT.Silu, norm_high)
            mixer2(nb + FFN_UNITS)
            nb += FFN_UNITS + M2_UNITS
            ffn(nb, ACT.Gelu_apprx_tanh, norm_high)

        @block.tensor
        def _(pe):
            def product(dst, w, cols, hi, lo, first, last):
                wh, wl = w[0][:, cols], w[1][:, cols]
                pe.matmul(dst, wh, hi, start=first, stop=False)
                pe.matmul(dst, wh, lo, start=False, stop=False)
                return pe.matmul(dst, wl, hi, start=False, stop=last)

            def unit(nb, it, K, M, hi, lo, ready=None, between={}):
                s = nb % 2
                pe.wait_ge(w_lo, nb + 1 + 2 * it)
                if not (isinstance(it, int) and nb + 2 * it < 2):
                    pe.wait_ge(evac[s], nb // 2 + it)
                for k in range(K):
                    for job in between.get(k, ()):
                        job()
                    if ready:
                        ready(k)
                    for m in range(M):
                        at = (k * M + m) * P
                        last = product(DB[s][m][:, :], (whi[s], wlo[s]), slice(at, at + P),
                                       hi[:, k, :], lo[:, k, :], k == 0, k == K - 1)
                last.then_inc(pe_done, 1)

            nacc = Tally(acc_ready)
            ndiag = Tally(diag_ready)

            def norm():
                pe.wait_ge(acc_ready, nacc.step())
                for c in range(4):
                    last = pe.matmul(XB[0][:, c:c + 1], acc[:, c * P:(c + 1) * P], ones[:, 0:1],
                                     start=True, stop=True)
                last.then_inc(sums_out, 1)
                pe.wait_ge(diag_ready, ndiag.step())
                for c in range(4):
                    last = pe.matmul(XB[1][:, c * P:(c + 1) * P], ones[:, :], diag[:, c, :],
                                     start=True, stop=True)
                last.then_inc(spread, 1)

            us = [0]

            def u_tile(k):
                pe.wait_ge(u_ready, us[0] + k + 1)

            hs = [0]

            def ffn(nb):
                for h, tiles in enumerate(HALVES):
                    def up_turn(it):
                        alone = isinstance(it, int)
                        for j in range(2):
                            unit(nb + j, it, KD, 2, uhi, ulo,
                                 u_tile if alone and j == 0 and h == 0 else None)

                    def down_turn(it):
                        alone = isinstance(it, int)
                        for j in range(2):
                            unit(nb + j, it, tiles, 1, hhi, hlo,
                                 (lambda k: pe.wait_ge(h_ready, hs[0] + k + 1)) if alone and j == 0 else None)
                    rolled(pe, tiles // 2, up_turn, [])
                    nb += tiles
                    rolled(pe, KD // 2, down_turn, [])
                    nb += KD
                    hs[0] += tiles
                us[0] += KD

            def mixer1(nb):
                def a_up():
                    pe.wait_ge(aup_in, 16)
                    pe.wait_ge(evac[nb % 2], nb // 2 + 1)
                    for m in range(2):
                        last = pe.matmul(XB[m][:, :], aup[:, m * P:(m + 1) * P], alow[:, :], start=True, stop=True)
                    last.then_inc(aup_out, 1)

                def v_unit(i):
                    s = (nb + i) % 2
                    pe.wait_ge(w_lo, nb + i + 1)
                    pe.wait_ge(evac[s], (nb + i) // 2)
                    for t in range(PAIRS):
                        dst = DB[s][t // 2][:, (t % 2) * 2 * P:(t % 2 + 1) * 2 * P]
                        tok = slice(t * P, (t + 1) * P)
                        for k in range(KD):
                            cols = slice(k * 2 * P, (k + 1) * 2 * P)
                            pe.matmul(dst, uhi[:, k, tok], whi[s][:, cols], start=k == 0, stop=False)
                            pe.matmul(dst, uhi[:, k, tok], wlo[s][:, cols], start=False, stop=False)
                            last = pe.matmul(dst, ulo[:, k, tok], whi[s][:, cols], start=False, stop=k == KD - 1)
                    last.then_inc(pe_done, 1)

                def turn_kend():
                    pe.wait_ge(gla_in, 1)
                    for p in range(PAIRS):
                        for g in range(2):
                            at = ((p % 2) * 2 + g) * P
                            last = pe.transpose(XB[p // 2][:, at:at + P], k_f[:, g, p * P:(p + 1) * P], ident[:, :])
                    last.then_inc(kend_out, 1)

                def head(h):
                    return h // 2, slice(DK * (h % 2), DK * (h % 2) + DK)

                def q_of(h):
                    return eq if h % 2 else q_f

                def scores(p):
                    pe.wait_ge(kend_in, 2)
                    if p:
                        pe.wait_ge(yg_ready, p)
                    tok = slice(p * P, (p + 1) * P)
                    for h in range(4):
                        g, rows = head(h)
                        last = pe.matmul(XB[2][:, h * P:(h + 1) * P], ek[:, g, tok], q_of(h)[:, g, tok],
                                         start=True, stop=True)
                    last.then_inc(scores_out, 1)
                    if p:
                        pe.wait_ge(state_in, p)
                    for c in range(2):
                        rows_t = slice(c * CHUNK, (c + 1) * CHUNK)
                        for h in range(4):
                            g, rows = head(h)
                            last = pe.matmul(XB[c][rows, g * P:(g + 1) * P],
                                             kend_t[rows_t, p, g, rows], v_t[rows_t, p, h * DV:(h + 1) * DV],
                                             start=True, stop=True)
                    last.then_inc(dstate_out, 1)

                def outputs(p):
                    pe.wait_ge(masked, p + 1)
                    pe.wait_ge(state_in, p + 1)
                    if p:
                        pe.wait_ge(o_kept, p)
                    for h in range(4):
                        g, rows = head(h)
                        pe.matmul(XB[3][:, h * P:(h + 1) * P], v_t[:, p, h * DV:(h + 1) * DV],
                                  s_t[:, p % 2, h, :], start=True, stop=False)
                        for c in range(2):
                            at = h * P + c * CHUNK
                            tok = slice(p * P + c * CHUNK, p * P + (c + 1) * CHUNK)
                            last = pe.matmul(XB[3][:, at:at + CHUNK], st[:, g, 2 * p + c, :],
                                             q_of(h)[:, g, tok], start=False, stop=c == 1)
                    last.then_inc(o_out, 1)

                def o_sums(p):
                    pe.wait_ge(o_kept, p + 1)
                    for h in range(4):
                        last = pe.matmul(XB[2][:, h:h + 1], ut[:, 1, h * P:(h + 1) * P], ones[:, 0:1],
                                         start=True, stop=True)
                    last.then_inc(sums_out, 1)

                def o_spread(p):
                    pe.wait_ge(diag_ready, ndiag.step())
                    for h in range(4):
                        last = pe.matmul(XB[2][:, h * P:(h + 1) * P], ones[:, :], diag[:, h, :], start=True, stop=True)
                    last.then_inc(spread, 1)

                def drive(j):
                    q = j % 2
                    pe.wait_ge(side5_in[q], 32 * (j // 2 + 1))
                    if j == 0:
                        s = (nb + M1["s5"] + 1) % 2
                        pe.wait_ge(evac[s], (nb + M1["s5"] + 1) // 2 + 1)
                        pe.wait_ge(yg_ready, PAIRS)
                    else:
                        pe.wait_ge(bu_read, j)
                    for c in range(2):
                        last = pe.matmul(XB[c][:, :], bc5[:, q, c * P:(c + 1) * P], s5in[:, j // 4, :],
                                         start=True, stop=True)
                    last.then_inc(bu_out, 1)

                def read_out(j):
                    q, m = j % 2, j // 4
                    pe.wait_ge(re_ready, j + 1)
                    pe.wait_ge(im_ready, j + 1)
                    pe.wait_ge(c5_ready, j + 1)
                    if j % 4 == 0 and m >= 2:
                        pe.wait_ge(z_sum, m - 1)
                    pe.matmul(XB[2 + m % 2][:, :], c5[:, q, 0:P], state5[:, q, 0, :], start=j % 4 == 0, stop=False)
                    pe.matmul(XB[2 + m % 2][:, :], c5[:, q, P:2 * P], state5[:, q, 1, :], start=False,
                              stop=j % 4 == 3).then_inc(y5_out, 1)

                between = {i: {} for i in range(M1_UNITS)}
                between[1][4] = [a_up]
                between[5][2] = [turn_kend]
                for p in range(PAIRS):
                    for k, job in ((0, scores), (3, outputs), (5, o_sums), (7, o_spread)):
                        between[6 + p][k] = [lambda job=job, p=p: job(p)]
                for j in range(T5 + 2):
                    i, k = slot5(j)
                    here = between[i].setdefault(k, [])
                    if j < T5:
                        here.append(lambda j=j: drive(j))
                    if j >= 2:
                        here.append(lambda j=j: read_out(j - 2))

                norm()
                for i in range(M1_UNITS):
                    if M1["v"] <= i < M1["v"] + 2:
                        v_unit(i)
                    elif i < M1["pgla"]:
                        unit(nb + i, 0, KD, 1 if i == 0 else 2, uhi, ulo, u_tile if i == 0 else None, between[i])
                    elif i < M1["glu"]:
                        unit(nb + i, 0, 4, 2, yg_hi, yg_lo, None, between[i])
                    elif i < M1["ps5"]:
                        unit(nb + i, 0, 4, 2, z_hi, z_lo, (lambda k: pe.wait_ge(z_ready, k + 1)))
                    elif i < M1["wout"]:
                        unit(nb + i, 0, 4, 2, ys_hi, ys_lo, (lambda k: pe.wait_ge(ys_ready, k + 1)))
                    else:
                        unit(nb + i, 0, KD, 2, uhi, ulo, u_tile if i == M1["wout"] else None)
                    if i == 0 or i == M1["wout"]:
                        us[0] += KD

            pe.wait_ge(const_made, 1)
            def mixer2(nb):
                def head_gates(h):
                    q = h % 2
                    pe.wait_ge(wg_in[q], 16 * (h // 2 + 1))
                    pe.wait_ge(xa_ready, HEADS)
                    if h:
                        pe.wait_ge(lru_gates, h)
                    for n in range(4):
                        last = pe.matmul(XB[n][:, :], wg[q][:, n, :], xa[:, h, :],
                                         start=True, stop=True)
                    last.then_inc(lru_out, 1)

                norm()
                norm()
                for i in range(M2_UNITS):
                    name, u = M2_KIND[i]
                    side = {0: [lambda: head_gates(i - LRU_AT)]} if 0 <= i - LRU_AT < HEADS else {}
                    if name in ("ua", "ub", "ga", "gb"):
                        unit(nb + i, 0, KD, 2, uhi, ulo, u_tile if i == 0 else None, side)
                    elif name == "wp":
                        unit(nb + i, 0, 2, 2, pool_hi[:, u % 2, :, :], pool_lo[:, u % 2, :, :],
                             lambda k: pe.wait_ge(pooled, 2 * u + k + 1))
                    elif name == "pb":
                        unit(nb + i, 0, KD, 2, t_hi, t_lo, lambda k: pe.wait_ge(t_ready, k + 1), side)
                    elif name == "pa":
                        unit(nb + i, 0, HEADS, 1, ya_hi, ya_lo, lambda k: pe.wait_ge(ya_ready, k + 1))
                    else:
                        unit(nb + i, 0, KD, 2, uhi, ulo, u_tile if u == 0 else None)
                    if i == 0 or i == M2["wout"][0]:
                        us[0] += KD

            norm()
            ffn(0)
            mixer1(FFN_UNITS)
            nb = FFN_UNITS + M1_UNITS
            norm()
            ffn(nb)
            mixer2(nb + FFN_UNITS)
            nb += FFN_UNITS + M2_UNITS
            norm()
            ffn(nb)
            norm()

        @block.vector
        def _(dve):
            steps = Tally(dve_step)

            def then(ins):
                ins.then_inc(dve_step, 1)
                dve.wait_ge(dve_step, steps.step())

            def col(name, k=0):
                c = VECS[name] + k
                return vec[:, c:c + 1]

            def square_in(k):
                then(dve.tensor_tensor(out=sq[:, :], in0=x[:, k, :], in1=x[:, k, :], op=ALU.mult))
                then(dve.tensor_tensor(out=acc[:, :], in0=acc[:, :], in1=sq[:, :], op=ALU.add))

            n_norm = Tally(sums_out)
            n_rs = Tally(rs_ready)
            n_spread = Tally(spread)

            def root(sums=None, over=D):
                if sums is None:
                    dve.engine_nop().then_inc(acc_ready, 1)
                    sums = XB[0][:, 0:4]
                dve.wait_ge(sums_out, n_norm.step())
                dve.tensor_scalar(nstat[:, 0:4], sums, 1.0 / over, EPS, ALU.mult, ALU.add).then_inc(rt_ready, 1)
                dve.wait_ge(rs_ready, n_rs.step())
                for c in range(4):
                    last = dve.tensor_scalar(diag[:, c, :], ident[:, :], nstat[:, 4 + c:5 + c], None, ALU.mult)
                last.then_inc(diag_ready, 1)
                dve.wait_ge(spread, n_spread.step())

            n_uhi = Tally(uhi_ready)
            n_u = [0]

            def norm(gain):
                root()

                def lower(k):
                    dve.wait_ge(uhi_ready, n_uhi.step())
                    dve.tensor_tensor(out=ulo[:, k, :], in0=ut[:, k % 2, :], in1=uhi[:, k, :].bitcast(F32),
                                      op=ALU.subtract).then_inc(u_ready, 1)
                    n_u[0] += 1
                for k in range(KD):
                    if k >= 2:
                        dve.wait_ge(u_ready, n_u[0])
                    dve.scalar_tensor_tensor(out=ut[:, k % 2, :], in0=x[:, k, :], scalar=col(gain, k),
                                             in1=XB[1][:, :], op0=ALU.mult, op1=ALU.mult).then_inc(ut_ready, 1)
                    if k >= 1:
                        lower(k - 1)
                lower(KD - 1)

            def norm_x(gain, ready=None):
                root()
                then(dve.memset(acc[:, :], 0.0))
                for k in range(KD):
                    ins = dve.scalar_tensor_tensor(out=x[:, k, :], in0=x[:, k, :], scalar=col(gain, k),
                                                   in1=XB[1][:, :], op0=ALU.mult, op1=ALU.mult)
                    if ready:
                        ins.then_inc(ready, 1)
                    else:
                        then(ins)
                        square_in(k)

            gates = Tally(act_tile)
            n_h = Tally(h_ready)

            def split_h(src, m):
                then(dve.tensor_copy(hhi[:, m, :], src))
                dve.tensor_tensor(out=hlo[:, m, :], in0=src, in1=hhi[:, m, :].bitcast(F32),
                                  op=ALU.subtract).then_inc(h_ready, 1)

            def up_tile(nb, it, m):
                s = nb % 2
                dve.wait_ge(act_tile, gates.step())
                dve.tensor_tensor(out=ht[:, s, :], in0=DB[s][1][:, :], in1=sil[:, s, :], op=ALU.mult)\
                   .then_inc(evac[s], 1)
                dve.wait_ge(evac[s], nb // 2 + 1 + it)

            n_sines = Tally(sines)
            n_out = [Tally(trig_out[0]), Tally(trig_out[1])]

            def turns_of(h, it):
                for j in range(2):
                    tile = KD * h + 2 * it + j
                    hi, lo = v5[:, 12, bass.ds(tile, 1)], v5[:, 13, bass.ds(tile, 1)]
                    then(dve.tensor_scalar(turn_t[:, j, :], steps5[:, :], hi, ROUND, ALU.mult, ALU.add))
                    then(dve.tensor_scalar(turn_t[:, j, :], turn_t[:, j, :], ROUND, None, ALU.subtract))
                    then(dve.scalar_tensor_tensor(out=turn_t[:, j, :], in0=steps5[:, :], scalar=hi,
                                                  in1=turn_t[:, j, :], op0=ALU.mult, op1=ALU.subtract))
                    dve.scalar_tensor_tensor(out=turn[:, j, :], in0=steps5[:, :], scalar=lo, in1=turn_t[:, j, :],
                                             op0=ALU.mult, op1=ALU.add).then_inc(turned, 1)

            def trig_from(it):
                for j in range(2):
                    dve.wait_ge(sines, n_sines.step())
                    if not isinstance(it, int) or trig_slot_used[0]:
                        dve.wait_ge(trig_out[j], n_out[j].step(16))
                    dve.tensor_scalar(trig[:, j, 0:S], turn_q[:, j, :], -1.0, 1.0, ALU.mult, ALU.add)
                    dve.scalar_tensor_tensor(out=trig[:, j, S:2 * S], in0=turn_s[:, j, :], scalar=2.0,
                                             in1=turn_c[:, j, :], op0=ALU.mult, op1=ALU.mult).then_inc(trig_ready, 1)

            trig_slot_used = [False]

            def conv_tile(nb, it, m):
                s = nb % 2
                dve.wait_ge(pe_done, nb + 1 + 2 * it)
                for half, dst in ((0, cva), (1, cvb)):
                    src = DB[s][half]
                    tap = [vec[:, bass.ds(VECS["conv_f_w_2"] + 44 * k + 22 * half + m, 1)] for k in range(3)]
                    bias = vec[:, bass.ds(VECS["conv_f_b_2"] + 22 * half + m, 1)]
                    then(dve.tensor_scalar(dst[:, s, :], src[:, :], tap[1], bias, ALU.mult, ALU.add))
                    then(dve.scalar_tensor_tensor(out=dst[:, s, 1:S], in0=src[:, 0:S - 1], scalar=tap[0],
                                                  in1=dst[:, s, 1:S], op0=ALU.mult, op1=ALU.add))
                    dve.scalar_tensor_tensor(out=dst[:, s, 0:S - 1], in0=src[:, 1:S], scalar=tap[2],
                                             in1=dst[:, s, 0:S - 1], op0=ALU.mult, op1=ALU.add)\
                       .then_inc(evac[s] if half else conv_done, 1)
                dve.wait_ge(evac[s], nb // 2 + 1 + it)
                dve.wait_ge(act_tile, gates.step())
                then(dve.tensor_tensor(out=ht[:, s, :], in0=cvb[:, s, :], in1=sil[:, s, :], op=ALU.mult))

            def ffn(nb, tile, trig_of=False, share=0.5):
                for h, tiles in enumerate(HALVES):
                    def up_turn(it):
                        for j in range(2):
                            tile(nb + j, it, 2 * it + j + sum(HALVES[:h]))
                            split_h(ht[:, (nb + j) % 2, :], 2 * it + j)

                    def down_turn(it):
                        if trig_of:
                            turns_of(h, it)
                        for j in range(2):
                            if trig_of and j:
                                trig_from(it)
                            s, m = (nb + j) % 2, 2 * it + j
                            dve.wait_ge(pe_done, nb + j + 1 + 2 * it)
                            dve.scalar_tensor_tensor(out=x[:, m, :], in0=DB[s][0][:, :], scalar=share,
                                                     in1=x[:, m, :], op0=ALU.mult, op1=ALU.add).then_inc(evac[s], 1)
                            if h == 1:
                                dve.wait_ge(evac[s], (nb + j) // 2 + 1 + it)
                                square_in(m)
                    rolled(dve, tiles // 2, up_turn, [gates, steps])
                    nb += tiles
                    if h == 1:
                        then(dve.memset(acc[:, :], 0.0))
                    if trig_of and h == 0:
                        down_turn(0)
                        trig_slot_used[0] = True
                        rolled_on(dve, 1, KD // 2, down_turn, [steps, n_sines, n_out[0], n_out[1]])
                    else:
                        rolled(dve, KD // 2, down_turn, [steps, n_sines, n_out[0], n_out[1]])
                    nb += KD

            LRE, LIM, DT = (vec[:, VECS[n]:VECS[n] + T5] for n in ("lam_re", "lam_im", "log_dt"))

            def small5():
                tt, ts, stt = dve.tensor_tensor, dve.tensor_scalar, dve.scalar_tensor_tensor

                def v(i):
                    return v5[:, i, :]
                dve.wait_ge(s5_exp, 1)
                then(tt(out=v(1), in0=LRE, in1=v(0), op=ALU.mult))
                then(tt(out=v(3), in0=LIM, in1=v(0), op=ALU.mult))
                then(ts(v(2), v(3), 1.0 / TAU, ROUND, ALU.mult, ALU.add))
                then(ts(v(2), v(2), ROUND, None, ALU.subtract))
                for part in (TAU_1, TAU_2, TAU_3):
                    then(stt(out=v(3), in0=v(2), scalar=-part, in1=v(3), op0=ALU.mult, op1=ALU.add))
                dve.engine_nop().then_inc(s5_angle, 1)
                dve.wait_ge(s5_exp, 2)
                then(tt(out=v(7), in0=v(5), in1=v(5), op=ALU.mult))
                then(ts(v(7), v(7), -2.0, 1.0, ALU.mult, ALU.add))
                then(stt(out=v(8), in0=v(5), scalar=2.0, in1=v(6), op0=ALU.mult, op1=ALU.mult))
                then(tt(out=v(7), in0=v(7), in1=v(1), op=ALU.mult))
                then(tt(out=v(8), in0=v(8), in1=v(1), op=ALU.mult))
                then(ts(v(7), v(7), 1.0, None, ALU.subtract))
                then(tt(out=v(10), in0=LRE, in1=LRE, op=ALU.mult))
                then(tt(out=v(11), in0=LIM, in1=LIM, op=ALU.mult))
                then(tt(out=v(10), in0=v(10), in1=v(11), op=ALU.add))
                then(dve.reciprocal(v(10), v(10)))
                then(tt(out=v(11), in0=v(7), in1=LRE, op=ALU.mult))
                then(tt(out=v(12), in0=v(8), in1=LIM, op=ALU.mult))
                then(tt(out=v(11), in0=v(11), in1=v(12), op=ALU.add))
                then(tt(out=v(12), in0=v(8), in1=LRE, op=ALU.mult))
                then(tt(out=v(13), in0=v(7), in1=LIM, op=ALU.mult))
                then(tt(out=v(12), in0=v(12), in1=v(13), op=ALU.subtract))
                then(tt(out=v(7), in0=v(11), in1=v(10), op=ALU.mult))
                then(tt(out=v(8), in0=v(12), in1=v(10), op=ALU.mult))
                then(ts(v(9), v(8), -1.0, None, ALU.mult))
                then(ts(v(11), v(3), 1.0 / TAU, None, ALU.mult))
                then(ts(v(12), v(11), ROUND13, ROUND13, ALU.add, ALU.subtract))
                then(tt(out=v(13), in0=v(11), in1=v(12), op=ALU.subtract))

            def small_lru():
                tt, ts, stt = dve.tensor_tensor, dve.tensor_scalar, dve.scalar_tensor_tensor

                def v(i):
                    return lam[:, i, :]
                lams = vec[:, VECS["lam_f_2"]:VECS["lam_f_2"] + 2 * HEADS]
                dve.wait_ge(lam_exp, 1)
                then(ts(v(3), v(2), 2.0, None, ALU.add))
                then(dve.reciprocal(v(3), v(3)))
                then(tt(out=v(2), in0=v(2), in1=v(3), op=ALU.mult))
                then(tt(out=v(3), in0=v(2), in1=v(2), op=ALU.mult))
                then(ts(v(4), v(3), 1.0 / 15, 1.0 / 13, ALU.mult, ALU.add))
                for n in (11, 9, 7, 5, 3, 1):
                    then(tt(out=v(4), in0=v(4), in1=v(3), op=ALU.mult))
                    then(ts(v(4), v(4), 1.0 / n, None, ALU.add))
                then(stt(out=v(4), in0=v(4), scalar=2.0, in1=v(2), op0=ALU.mult, op1=ALU.mult))
                then(ts(v(3), lams, -1.0, 0.0, ALU.mult, ALU.max))
                then(tt(out=v(4), in0=v(4), in1=v(3), op=ALU.add))
                ts(v(0), v(4), LRU_C, None, ALU.mult)
                then(ts(v(1), v(4), -LRU_C, None, ALU.mult))

            def mixer2(nb):
                tt, ts, stt = dve.tensor_tensor, dve.tensor_scalar, dve.scalar_tensor_tensor

                def bank_of(i, m):
                    return DB[(nb + i) % 2][m][:, :]

                def done(i):
                    dve.wait_ge(pe_done, nb + i + 1)

                def freed(i, ins):
                    s = (nb + i) % 2
                    ins.then_inc(evac[s], 1)
                    dve.wait_ge(evac[s], (nb + i) // 2 + 1)

                def split(hi, lo, src, ready):
                    then(dve.tensor_copy(hi, src))
                    tt(out=lo, in0=src, in1=hi.bitcast(F32), op=ALU.subtract).then_inc(ready, 1)

                def conv_in(u):
                    i = M2["ua"][u]
                    done(i)
                    for m in range(2):
                        n = 2 * u + m
                        src, dst = bank_of(i, m), xa[:, n, :]
                        tap = [col("conv_a_w_2", HEADS * k + n) for k in range(4)]
                        then(ts(dst, src, tap[2], col("conv_a_b_2", n), ALU.mult, ALU.add))
                        for k, off in ((0, 2), (1, 1)):
                            then(stt(out=dst[:, off:S], in0=src[:, 0:S - off], scalar=tap[k], in1=dst[:, off:S],
                                     op0=ALU.mult, op1=ALU.add))
                        ins = stt(out=dst[:, 0:S - 1], in0=src[:, 1:S], scalar=tap[3], in1=dst[:, 0:S - 1],
                                  op0=ALU.mult, op1=ALU.add)
                        if m:
                            freed(i, ins)
                        else:
                            then(ins)
                    dve.engine_nop().then_inc(xa_ready, 2)

                def windows(g):
                    i = M2["ub"][g]
                    done(i)
                    for m in range(2):
                        ins = dve.tensor_copy(win[0][:, EDGE:EDGE + S], bank_of(i, m))
                        if m:
                            freed(i, ins)
                        else:
                            then(ins)
                        src, end = win[0], S + 2 * EDGE
                        then(tt(out=win[1][:, 1:end], in0=src[:, 0:end - 1], in1=src[:, 1:end], op=ALU.add))
                        have, lost, now, other = 2, 1, win[1], win[2]
                        while have < WINDOWS[g]:
                            d = have // 2
                            then(tt(out=other[:, lost + d:end - d], in0=now[:, lost:end - 2 * d],
                                    in1=now[:, lost + 2 * d:end], op=ALU.add))
                            have, lost, end, now, other = 2 * have, lost + d, end - d, other, now
                        mean = other[:, 0:S]
                        sums, tok = now[:, EDGE:EDGE + S], src[:, EDGE:EDGE + S]
                        then(stt(out=mean, in0=sums, scalar=1.0 / WINDOWS[g], in1=tok, op0=ALU.mult,
                                 op1=ALU.subtract))
                        for side, at in ((0, 0), (1, S - EDGE)):
                            part = mean[:, at:at + EDGE]
                            then(tt(out=part, in0=sums[:, at:at + EDGE],
                                    in1=per_count[:, g, side * EDGE:(side + 1) * EDGE], op=ALU.mult))
                            then(tt(out=part, in0=part, in1=tok[:, at:at + EDGE], op=ALU.subtract))
                        split(pool_hi[:, g % 2, m, :], pool_lo[:, g % 2, m, :], mean, pooled)
                        dve.wait_ge(pooled, 2 * g + m + 1)

                def pool_out(g):
                    i = M2["wp"][g]
                    done(i)
                    for m in range(2):
                        n = 2 * g + m
                        ins = ts(sq[:, :], bank_of(i, m), col("b_pool_2", n), col("pool_scale_2", n),
                                 ALU.add, ALU.mult)
                        if m:
                            freed(i, ins)
                        else:
                            then(ins)
                        split(t_hi[:, n, :], t_lo[:, n, :], sq[:, :], t_ready)
                        dve.wait_ge(t_ready, n + 1)

                def pool_branch(u):
                    i = M2["pb"][u]
                    done(i)
                    for m in range(2):
                        last = tt(out=gate_b[:, 2 * u + m, :], in0=bank_of(i, m), in1=gate_b[:, 2 * u + m, :],
                                  op=ALU.mult)
                    freed(i, last)

                def lru_inputs(h):
                    q = h % 2
                    for d in range(2):
                        dve.wait_ge(lru_exp, 2 * h + d + 1)
                        then(tt(out=sq[:, :], in0=lru_a[:, q, d, :], in1=lru_a[:, q, d, :], op=ALU.mult))
                        stt(out=lru_v[:, q, d, :], in0=sq[:, :], scalar=1.0, in1=lru_v[:, q, d, :],
                            op0=ALU.add, op1=ALU.mult).then_inc(lru_var, 1)
                        dve.wait_ge(lru_var, 2 * h + d + 1)
                        last = tt(out=lru_i[:, q, d, :], in0=lru_i[:, q, d, :], in1=xa[:, h, :], op=ALU.mult)
                    then(last)

                def lru_scans(h):
                    q = h % 2
                    for d, way in ((0, slice(None)), (1, slice(None, None, -1))):
                        b = lru_v[:, q, d, :]
                        dve.wait_ge(lru_root, 2 * h + d + 1)
                        then(tt(out=b, in0=b, in1=lru_i[:, q, d, :], op=ALU.mult))
                        b = lru_v[:, q, d, way]
                        last = dve.tensor_tensor_scan(b, lru_a[:, q, d, way], b, 0.0, ALU.mult, ALU.add)
                    then(last)
                    then(tt(out=acc[:, :], in0=lru_v[:, q, 0, :], in1=lru_v[:, q, 1, :], op=ALU.add))
                    split(ya_hi[:, h, :], ya_lo[:, h, :], acc[:, :], ya_ready)
                    dve.wait_ge(ya_ready, h + 1)

                def merge(u):
                    i = M2["pa"][u]
                    done(i)
                    freed(i, tt(out=sq[:, :], in0=bank_of(i, 0), in1=gate_a[:, u, :], op=ALU.mult))
                    then(tt(out=sq[:, :], in0=sq[:, :], in1=gate_b[:, u, :], op=ALU.add))
                    split(uhi[:, u, :], ulo[:, u, :], sq[:, :], u_ready)
                    n_u[0] += 1
                    dve.wait_ge(u_ready, n_u[0])

                def residual(u):
                    i = M2["wout"][u]
                    done(i)
                    for n in range(2):
                        m = 2 * u + n
                        ins = tt(out=x[:, m, :], in0=bank_of(i, n), in1=x[:, m, :], op=ALU.add)
                    freed(i, ins)
                    for n in range(2):
                        square_in(2 * u + n)

                norm_x("final_norm")
                dve.engine_nop().then_inc(x_done, 1)
                norm("g_mix_2")
                dve.wait_ge(spilled, 2 * 16 * KD)
                for u in range(len(M2["ua"])):
                    conv_in(u)
                for w in win:
                    last = dve.memset(w[:, :], 0.0)
                then(last)
                windows(0)
                windows(1)
                pool_out(0)
                windows(2)
                pool_out(1)
                windows(3)
                pool_out(2)
                pool_out(3)
                for h in range(HEADS + 1):
                    if h < HEADS:
                        lru_inputs(h)
                    if h:
                        lru_scans(h - 1)
                    u = h + LRU_AT - M2["pb"][0]
                    if 0 <= u < 4:
                        pool_branch(u)
                for u in range(KD):
                    merge(u)
                then(dve.memset(acc[:, :], 0.0))
                dve.wait_ge(x_back, 2 * 16 * KD)
                for u in range(4):
                    residual(u)

            def mixer1(nb):
                tt, ts, stt = dve.tensor_tensor, dve.tensor_scalar, dve.scalar_tensor_tensor

                def bank_of(i, m):
                    return DB[(nb + i) % 2][m][:, :]

                def done(i):
                    dve.wait_ge(pe_done, nb + i + 1)

                def freed(i, ins):
                    s = (nb + i) % 2
                    ins.then_inc(evac[s], 1)
                    dve.wait_ge(evac[s], (nb + i) // 2 + 1)

                def copy_out(i, dst, scale=None):
                    done(i)
                    for m in range(2):
                        last = ts(dst[:, m, :], bank_of(i, m), scale, None, ALU.mult) if scale else \
                            dve.tensor_copy(dst[:, m, :], bank_of(i, m))
                    freed(i, last)

                def values(u):
                    i = M1["v"] + u
                    done(i)
                    for half in range(2):
                        last = dve.tensor_copy(v_t[:, 2 * half:2 * half + 2, u * 2 * P:(u + 1) * 2 * P],
                                               bank_of(i, half).rearrange("p (t n) -> p t n", t=2))
                    freed(i, last)

                def gated_r(u):
                    dve.wait_ge(r_ready, 2 * (u + 1))
                    for m in (2 * u, 2 * u + 1):
                        last = ts(r_f[:, m, :], r_f[:, m, :], col("gla_out_norm", m), None, ALU.mult)
                    then(last)

                def pair(p):
                    dve.wait_ge(scores_out, p + 1)
                    then(dve.memset(s_t[:, p % 2, :, :], 0.0))
                    dve.copy_predicated(s_t[:, p % 2, :, :], causal[:, :].bitcast(U32).unsqueeze(1)
                                        .broadcast_to([P, 4, P]), XB[2][:, :].rearrange("p (h q) -> p h q", h=4))\
                       .then_inc(masked, 1)
                    dve.wait_ge(dstate_out, p + 1)
                    for c in range(2):
                        n = 2 * p + c
                        for g in range(2):
                            last = stt(out=st[:, g, n + 1, :], in0=st[:, g, n, :], scalar=decay[:, g, n:n + 1],
                                       in1=XB[c][:, g * P:(g + 1) * P],
                                       op0=ALU.mult, op1=ALU.add)
                        if c == 0:
                            then(last)
                    last.then_inc(state_in, 1)
                    dve.wait_ge(state_in, p + 1)
                    root(XB[2][:, 0:4], DV)

                def pair_out(p):
                    tok = slice(p * P, (p + 1) * P)
                    then(tt(out=sq[:, :], in0=ut[:, 0, :], in1=XB[2][:, :], op=ALU.mult))
                    y = sq[:, :].rearrange("p (h q) -> p h q", h=4)
                    then(tt(out=y, in0=y, in1=r_f[:, :, tok], op=ALU.mult))
                    then(dve.tensor_copy(yg_hi[:, :, tok], y))
                    tt(out=yg_lo[:, :, tok], in0=y, in1=yg_hi[:, :, tok].bitcast(F32), op=ALU.subtract)\
                        .then_inc(yg_ready, 1)
                    dve.wait_ge(yg_ready, p + 1)

                def state_tile(j):
                    q = j % 2
                    cos, sin = trig5[:, q, 0:S], trig5[:, q, S:2 * S]
                    wr, wi = rot[:, q, 0, :], rot[:, q, 1, :]
                    dve.wait_ge(side5_in[q], 32 * (j // 2 + 1))
                    dve.wait_ge(bu_out, j + 1)
                    if j >= 2:
                        dve.wait_ge(im_ready, j - 1)
                    tt(out=wr, in0=XB[0][:, :], in1=cos, op=ALU.mult)
                    tt(out=sq[:, :], in0=XB[1][:, :], in1=sin, op=ALU.mult)
                    tt(out=wi, in0=XB[1][:, :], in1=cos, op=ALU.mult)
                    tt(out=acc[:, :], in0=XB[0][:, :], in1=sin, op=ALU.mult).then_inc(bu_read, 1)
                    dve.wait_ge(bu_read, j + 1)
                    tt(out=wr, in0=wr, in1=sq[:, :], op=ALU.add)
                    then(tt(out=wi, in0=wi, in1=acc[:, :], op=ALU.subtract))
                    mag = v5[:, 1, j:j + 1].broadcast_to([P, S])
                    for w in (wr, wi):
                        dve.tensor_tensor_scan(w, mag, w, 0.0, ALU.mult, ALU.add).then_inc(scanned, 1)
                    if j >= 2:
                        dve.wait_ge(y5_out, j - 1)
                    fr, fi, nfi = (v5[:, i, j:j + 1] for i in (7, 8, 9))
                    cr, ci = bc5[:, q, 2 * P:3 * P], bc5[:, q, 3 * P:4 * P]
                    ts(c5[:, q, 0:P], ci, fi, None, ALU.mult)
                    then(ts(c5[:, q, P:2 * P], ci, fr, None, ALU.mult))
                    stt(out=c5[:, q, 0:P], in0=cr, scalar=fr, in1=c5[:, q, 0:P], op0=ALU.mult, op1=ALU.subtract)
                    stt(out=c5[:, q, P:2 * P], in0=cr, scalar=nfi, in1=c5[:, q, P:2 * P],
                        op0=ALU.mult, op1=ALU.subtract).then_inc(c5_ready, 1)
                    dve.wait_ge(scanned, 2 * (j + 1))
                    tt(out=sq[:, :], in0=wr, in1=cos, op=ALU.mult)
                    then(tt(out=acc[:, :], in0=wi, in1=sin, op=ALU.mult))
                    tt(out=state5[:, q, 0, :], in0=sq[:, :], in1=acc[:, :], op=ALU.subtract).then_inc(re_ready, 1)
                    dve.wait_ge(re_ready, j + 1)

                def z_in(m):
                    dve.wait_ge(y5_out, 4 * (m + 1))
                    stt(out=z_f[:, m, :], in0=s5in[:, m, :], scalar=col("s5_d", m), in1=XB[2 + m % 2][:, :],
                        op0=ALU.mult, op1=ALU.add).then_inc(z_sum, 1)

                def z_split(m):
                    dve.wait_ge(z_act, m + 1)
                    then(dve.tensor_copy(z_hi[:, m, :], z_f[:, m, :]))
                    tt(out=z_lo[:, m, :], in0=z_f[:, m, :], in1=z_hi[:, m, :].bitcast(F32), op=ALU.subtract)\
                        .then_inc(z_ready, 1)

                def attention_branch(u):
                    i = M1["pgla"] + u
                    done(i)
                    for m in range(2):
                        g = gate[:, 8 + 2 * u + m, :]
                        last = tt(out=g, in0=bank_of(i, m), in1=g, op=ALU.mult)
                    freed(i, last)

                def glu(u):
                    i = M1["glu"] + u
                    for m in range(2):
                        n = 2 * u + m
                        dve.wait_ge(glu_act, n + 1)
                        tt(out=sq[:, :], in0=z_f[:, n, :], in1=ut[:, m, :], op=ALU.mult).then_inc(glu_used, 1)
                        dve.wait_ge(glu_used, n + 1)
                        then(dve.tensor_copy(ys_hi[:, n, :], sq[:, :]))
                        last = tt(out=ys_lo[:, n, :], in0=sq[:, :], in1=ys_hi[:, n, :].bitcast(F32), op=ALU.subtract)
                        last.then_inc(ys_ready, 1)
                        dve.wait_ge(ys_ready, n + 1)
                    dve.engine_nop().then_inc(evac[(nb + i) % 2], 1)

                def merge(i, m, a, b):
                    done(i)
                    for n in range(2):
                        ins = tt(out=sq[:, :], in0=bank_of(i, n), in1=a[:, m + n, :], op=ALU.mult)
                        if n:
                            freed(i, ins)
                        else:
                            then(ins)
                        then(tt(out=sq[:, :], in0=sq[:, :], in1=b[:, m + n, :], op=ALU.add))
                        then(dve.tensor_copy(uhi[:, m + n, :], sq[:, :]))
                        n_u[0] += 1
                        tt(out=ulo[:, m + n, :], in0=sq[:, :], in1=uhi[:, m + n, :].bitcast(F32),
                           op=ALU.subtract).then_inc(u_ready, 1)
                        dve.wait_ge(u_ready, n_u[0])

                def residual(i, m):
                    done(i)
                    for n in range(2):
                        ins = tt(out=x[:, m + n, :], in0=bank_of(i, n), in1=x[:, m + n, :], op=ALU.add)
                    freed(i, ins)
                    for n in range(2):
                        square_in(m + n)

                norm("mix_norm")
                done(0)
                freed(0, dve.tensor_copy(alow[:, :], bank_of(0, 0)))
                then(dve.memset(first_of_chunk[:, :], 1.0))
                then(dve.memset(first_of_chunk[:, ::CHUNK], 0.0))
                dve.wait_ge(aup_out, 1)
                for m in range(2):
                    ts(la[:, m, :], XB[m][:, :], col("gla_a_up_b", m), 0.0, ALU.add, ALU.min).then_inc(z_neg, 1)
                copy_out(M1["k"], k_f)
                dve.wait_ge(ln_out, 1)
                then(tt(out=la[:, :, :], in0=la[:, :, :], in1=lt[:, :, :], op=ALU.subtract))
                for m in range(2):
                    dve.tensor_tensor_scan(la[:, m, :], first_of_chunk[:, :], la[:, m, :], 0.0, ALU.mult, ALU.add)\
                       .then_inc(bcum, 1)
                copy_out(M1["q"], q_f, DK ** -0.5)
                dve.wait_ge(exps_out, 1)
                la4 = la[:, :, :].rearrange("p m (n c) -> p m n c", c=CHUNK)
                for m in range(2):
                    last = tt(out=lt[:, m, :].rearrange("p (n c) -> p n c", c=CHUNK),
                              in0=la4[:, m, :, CHUNK - 1:CHUNK].broadcast_to([P, NCH, CHUNK]),
                              in1=la4[:, m, :, :], op=ALU.subtract)
                last.then_inc(rest_ready, 1)
                dve.tensor_copy(decay[:, :, :], eq[:, :, CHUNK - 1::CHUNK])
                then(tt(out=ek[:, :, :], in0=k_f[:, :, :], in1=ek[:, :, :], op=ALU.mult))
                then(tt(out=eq[:, :, :], in0=q_f[:, :, :], in1=eq[:, :, :], op=ALU.mult))
                dve.memset(q_f[DK:P, :, :], 0.0)
                then(dve.tensor_copy(q_f[0:DK, :, :], eq[0:DK, :, :]))
                dve.memset(eq[0:DK, :, :], 0.0)
                dve.memset(st[:, :, 0, :], 0.0)
                dve.wait_ge(rest_exp, 1)
                tt(out=k_f[:, :, :], in0=k_f[:, :, :], in1=lt[:, :, :], op=ALU.mult).then_inc(gla_in, 1)
                values(0)
                values(1)
                gated_r(0)
                pair(0)
                gated_r(1)
                pair_out(0)
                for p in range(1, PAIRS):
                    pair(p)
                    pair_out(p)
                    if p == 1:
                        dve.wait_ge(spilled, 16 * KD)
                    if p < 3:
                        copy_out(M1["s5"] + p - 1, s5in[:, 2 * (p - 1):2 * p, :])
                for j in range(T5):
                    state_tile(j)
                    if j in (5, 9, 13):
                        z_in(j // 4 - 1)
                    if j in (7, 11, 15):
                        z_split(j // 4 - 1)
                attention_branch(0)
                z_in(3)
                attention_branch(1)
                z_split(3)
                attention_branch(2)
                attention_branch(3)
                glu(0)
                glu(1)
                for u in range(4):
                    merge(M1["ps5"] + u, 2 * u, gate, gate[:, 8:16, :])
                then(dve.memset(acc[:, :], 0.0))
                dve.wait_ge(x_back, 16 * KD)
                for u in range(4):
                    residual(M1["wout"] + u, 2 * u)

            then(dve.memset(acc[:, :], 0.0))
            for k in range(KD):
                dve.wait_ge(x_in, 16 * KD)
                square_in(k)
            dve.wait_ge(vec_in, 16)
            dve.wait_ge(const_made, 1)
            norm("ffn1_norm")
            small_lru()
            small5()
            ffn(0, up_tile, True)
            dve.engine_nop().then_inc(x_done, 1)
            mixer1(FFN_UNITS)
            nb = FFN_UNITS + M1_UNITS
            norm("ffn2_norm")
            ffn(nb, up_tile)
            mixer2(nb + FFN_UNITS)
            nb += FFN_UNITS + M2_UNITS
            norm("g_ffn_2")
            ffn(nb, conv_tile, share=1.0)
            norm_x("g_final_2", out_ready)


def tiles(w, m):
    k, n = w.shape
    return np.ascontiguousarray(w.reshape(k // P, P, n // (m * P), m * P).transpose(2, 1, 0, 3)
                                ).reshape(n // (m * P), P, -1)


def up_units(a, b):
    w = np.stack([a, b]).reshape(2, KD, P, FF // P, P)
    return np.ascontiguousarray(w.transpose(3, 2, 1, 0, 4)).reshape(FF // P, P, UNIT)


def b_and_c(g):
    out = np.zeros((T5, P, 4, P), np.float32)
    for j in range(T5):
        for q in range(2):
            grp = 2 * j + q
            f = slice(32 * (j % 4) + H5 * q, 32 * (j % 4) + H5 * (q + 1))
            n = slice(P5 * q, P5 * (q + 1))
            for i, name in enumerate(("s5_b_re", "s5_b_im")):
                out[j, f, i, n] = g[name][0, grp].T
            for i, name in enumerate(("s5_c_re", "s5_c_im")):
                out[j, n, 2 + i, f] = g[name][0, grp].T
    return out.reshape(T5, P, 4 * P)


def by_feature(v):
    return np.asarray(v, dtype=v.dtype).reshape(-1, P).T


def lay_out(inp):
    g = {k: np.asarray(v) for k, v in inp.items()}
    a = {}
    a["xT"] = np.ascontiguousarray(g["x"][0].T)
    v = np.zeros((P, N_VECS), np.float32)

    def vput(name, cols):
        v[:, VECS[name]:VECS[name] + cols.shape[1]] = cols
    for name in ("ffn1_norm", "mix_norm", "ffn2_norm", "final_norm", "g_mix_2", "g_ffn_2", "g_final_2",
                 "gla_a_up_b", "gla_out_norm", "s5_d", "s5_glu_b", "b_gate_2", "conv_a_w_2", "conv_a_b_2",
                 "ba_f_2", "bx_f_2", "lam_f_2", "ba_b_2", "bx_b_2", "lam_b_2", "b_pool_2", "pool_scale_2",
                 "conv_f_w_2", "conv_f_b_2"):
        vput(name, by_feature(g[name]))
    vput("lam_re", by_feature(g["s5_lambda_re"]))
    vput("lam_im", by_feature(g["s5_lambda_im"]))
    vput("log_dt", by_feature(np.repeat(g["s5_log_dt"].reshape(-1), 64)))
    a["vec"] = v
    cut = HALVES[0] * P
    up2 = g["w_up_2"][0]
    for n, (w1, w3, w2) in {"1": (g["ffn1_w1"][0], g["ffn1_w3"][0], "ffn1_w2"),
                            "2": (g["ffn2_w1"][0], g["ffn2_w3"][0], "ffn2_w2"),
                            "3": (up2[:, :FF], up2[:, FF:], "w_down_2")}.items():
        a["up" + n] = up_units(w1, w3)
        a[f"down{n}a"] = tiles(g[w2][0][:cut], 1)
        a[f"down{n}b"] = tiles(g[w2][0][cut:], 1)
    w = g["w_in"][0]
    at = np.cumsum([0, 512, 256, 256, 512, 512, 16, D, D])
    s5, q, k, v_, r, low, gs, gg = (w[:, at[i]:at[i + 1]] for i in range(8))
    a["win1"] = tiles(np.concatenate([k, q, v_, r, s5, gs, gg], 1), 2)
    a["win1_alow"] = tiles(np.pad(low, ((0, 0), (0, P - 16))), 1)
    a["aup"] = np.pad(g["gla_a_up_w"][0], ((0, P - 16), (0, 0)))
    a["bc5"] = b_and_c(g)
    a["glu"] = tiles(g["s5_glu_w"][0], 2)
    a["ps5"] = tiles(g["proj_s5"][0], 2)
    a["pgla"] = tiles(g["proj_gla"][0], 2)
    a["wout1"] = tiles(g["w_out"][0], 2)
    w = g["w_in_2"][0]
    ua, ub, ga, gb = (w[:, i:j] for i, j in ((0, 1280), (1280, 2304), (2304, 3328), (3328, 4352)))
    a["ua2"], a["ub2"], a["ga2"], a["gb2"] = (tiles(t, 2) for t in (ua, ub, ga, gb))
    a["wp2"] = np.ascontiguousarray(g["w_pool_2"][0].reshape(4, 2, P, 2 * P).transpose(0, 2, 1, 3)).reshape(4, P, -1)
    a["pb2"] = tiles(g["p_b_2"][0], 2)
    a["pa2"] = tiles(g["p_a_2"][0], 1)
    a["wout2"] = tiles(g["w_out_2"][0], 2)
    a["wg2"] = np.ascontiguousarray(np.stack([g[n][0] for n in ("wa_f_2", "wx_f_2", "wa_b_2", "wx_b_2")])
                                    .transpose(1, 2, 0, 3)).reshape(HEADS, P, 4 * P)
    return a


def kernel(**inputs):
    import concourse.bacc as bacc
    from concourse.bass_utils import run_bass_kernel_spmd

    nc = bacc.Bacc("TRN2", target_bir_lowering=False, num_devices=1)
    arrays = {"in_" + k: v for k, v in lay_out(inputs).items()}
    aps = {k[3:]: nc.dram_tensor(k, v.shape, mybir.dt.from_np(v.dtype), kind="ExternalInput").ap()
           for k, v in arrays.items()}
    out = nc.dram_tensor("out_xT", (D, S), F32, kind="ExternalOutput").ap()
    build(nc, aps, out)
    r = run_bass_kernel_spmd(nc, [arrays], core_ids=[0])
    return np.ascontiguousarray(r.results[0]["out_xT"].T)[None]
```

```python
import numpy as np
import concourse.bass as bass
from concourse import mybir
from contextlib import ExitStack

F32 = mybir.dt.float32
F32R = mybir.dt.float32r
U32 = mybir.dt.uint32
ALU = mybir.AluOpType
ACT = mybir.ActivationFunctionType

P = 128
S = 512
D = 1024
KD = D // P
FF = 2816
EPS = 1e-6
HALVES = (12, 10)
assert sum(HALVES) * P == FF
UNIT = 2048

FFN_UNITS = sum(HALVES) + 2 * KD

G5, P5, H5 = 32, 64, 16
T5 = G5 * P5 // P
ROUND = 1.5 * 2.0 ** 23
ROUND13 = 1.5 * 2.0 ** 10
TAU = 2.0 * np.pi
TAU_1 = 6.28125
TAU_2 = float(np.float32(np.round((TAU - TAU_1) * 2.0 ** 21) / 2.0 ** 21))
TAU_3 = float(np.float32(TAU - TAU_1 - TAU_2))

DV, DK, CHUNK = 128, 64, 64
NCH = S // CHUNK
PAIRS = S // P

M1 = {"alow": 0, "k": 1, "q": 2, "v": 3, "r": 5, "s5": 7, "gs": 9, "gg": 13, "pgla": 17, "glu": 21,
      "ps5": 23, "wout": 27}
M1_UNITS = 31
S5_FIRST, S5_EVERY = 4, 3.5
F5 = P // 4

HEADS = 10
LRU_C = 8.0
WINDOWS = (2, 4, 8, 16)
EDGE = max(WINDOWS) // 2

M2 = {"ua": (0, 1, 2, 3, 4), "ub": (5, 6, 7, 8), "gb": (9, 10, 12, 13), "wp": (11,),
      "pb": (14, 15, 16, 17), "ga": (18, 19, 20, 21), "pa": tuple(range(22, 30)), "wout": (30, 31, 32, 33)}
M2_UNITS = 34
M2_KIND = {i: (name, u) for name, at in M2.items() for u, i in enumerate(at)}
HEAD_EVERY, HEAD_FIRST, HEAD_LATE, SIDE_LATE = 6.5, 4, 6, 3


def head_slot(h):
    at = HEAD_FIRST + int(HEAD_EVERY * h)
    return M2["wp"][0] + 1 + at // KD, at % KD



class Tally:

    def __init__(self, sem):
        self.sem, self.base, self.local, self.turn, self.per = sem, 0, 0, None, 0

    def step(self, by=1):
        self.local += by
        return self.value()

    def value(self):
        if self.turn is None:
            return self.base + self.local
        return (self.turn - 1) * self.per + (self.base + self.local)


def rolled(eng, turns, body, tallies):
    before = [t.base + t.local for t in tallies]
    body(0)
    for t, b in zip(tallies, before):
        t.base, t.local = t.base + t.local, 0
        t.per = t.base - b
    with eng.Fori(1, turns) as it:
        for t in tallies:
            t.turn = it
        body(it)
    for t in tallies:
        assert t.local == t.per
        t.base, t.local, t.turn = t.base + (turns - 1) * t.per, 0, None


def rolled_on(eng, start, end, body, tallies):
    before = [t.base + t.local for t in tallies]
    body(start)
    for t, b in zip(tallies, before):
        t.base, t.local = t.base + t.local, 0
        t.per = t.base - b
    with eng.Fori(start + 1, end) as it:
        for t in tallies:
            t.turn = it - start
        body(it)
    for t in tallies:
        assert t.local == t.per
        t.base, t.local, t.turn = t.base + (end - start - 1) * t.per, 0, None


def head_turn(h):
    i, k = head_slot(h)
    return i + 1 + (k >= HEAD_LATE)


def columns(names_widths):
    at, out = 0, {}
    for name, width in names_widths:
        out[name] = at
        at += width
    return out, at


VECS, N_VECS = columns([("ffn1_norm", 8), ("mix_norm", 8), ("ffn2_norm", 8), ("final_norm", 8),
                        ("g_mix_2", 8), ("g_ffn_2", 8), ("g_final_2", 8),
                        ("gla_a_up_b", 2), ("gla_out_norm", 4), ("s5_d", 4), ("s5_glu_b", 4),
                        ("lam_re", 16), ("lam_im", 16), ("log_dt", 16),
                        ("b_gate_2", 16), ("conv_a_w_2", 40), ("conv_a_b_2", 10),
                        ("ba_f_2", 10), ("bx_f_2", 10),
                        ("ba_b_2", 10), ("bx_b_2", 10), ("lam_f_2", 10), ("lam_b_2", 10),
                        ("b_pool_2", 8), ("pool_scale_2", 8),
                        ("conv_f_w_2", 132), ("conv_f_b_2", 44)])


def build(nc, A, out):
    ctx = ExitStack()
    with ctx:
        def sem(name):
            return ctx.enter_context(nc.semaphore(name))

        top = [16512]

        def put(name, shape, dt=F32, at=None):
            size = 4 * int(np.prod(shape[1:]))
            if at is None:
                at, top[0] = top[0], top[0] + -(-size // 32) * 32
            t = nc.alloc_sbuf_tensor_at(name, shape, dt, offset=at)
            return t

        vec = put("vec", [P, N_VECS])
        ident = put("ident", [P, P])
        ones = put("ones", [P, P])
        acc = put("acc", [P, S])
        sq = put("sq", [P, S])
        squares = put("squares", [P, 2, S], at=top[0] - 2 * 4 * S)
        diag = put("diag", [P, 4, P])
        bc5_third = put("bc5_third", [P, 2 * P + 2 * F5], at=top[0] - 4 * 4 * P)
        ut = put("ut", [P, 2, S])
        nstat = put("nstat", [P, 16])
        inv_late = put("inv_late", [P, S], at=top[0])
        aup = put("aup", [P, 2 * P])
        causal = put("causal", [P, P])
        v5 = put("v5", [P, 14, T5])
        raw = [put(f"raw{i}", [P, UNIT]) for i in range(2)]
        whi = [put(f"whi{i}", [P, UNIT], F32R) for i in range(2)]
        wlo = [put(f"wlo{i}", [P, UNIT], F32R) for i in range(2)]
        lam_pi = put("lam_pi", [P, 5 * 2 * HEADS + 1])
        lam = lam_pi[:, 0:5 * 2 * HEADS].rearrange("p (i h) -> p i h", i=5)
        half_pi = lam_pi[:, 5 * 2 * HEADS:5 * 2 * HEADS + 1]
        per_count = put("per_count", [P, len(WINDOWS), 2 * EDGE])
        uhi = put("uhi", [P, KD, S], F32R)
        ulo = put("ulo", [P, KD, S], F32R)
        region = top[0]
        x = put("x", [P, KD, S])
        hhi = put("hhi", [P, max(HALVES), S], F32R)
        hlo = put("hlo", [P, max(HALVES), S], F32R)
        sil = put("sil", [P, 2, S])
        ht = put("ht", [P, 2, S])
        cva = put("cva", [P, 2, S])
        cvb = put("cvb", [P, 2, S])

        steps5 = put("steps5", [P, S])
        turn_t = put("turn_t", [P, 2, S])
        turn = put("turn", [P, 2, S])
        turn_c = put("turn_c", [P, 2, S])
        turn_s = put("turn_s", [P, 2, S])
        turn_q = put("turn_q", [P, 2, S])
        trig = put("trig", [P, 2, 2 * S])
        inv_first = put("inv_first", [P, S])
        assert top[0] <= 229344

        def at_kb(kb):
            return region + int(kb * 1024)

        acc_2 = put("acc_2", [P, S], at=at_kb(80))
        gains = put("gains", [P, 2, KD], at=at_kb(82))
        conv_src = put("conv_src", [P, 2, S], at=at_kb(84))

        cos5 = [put(f"cos5_{i}", [P, S], at=at_kb(kb)) for i, kb in enumerate((0, 2, 14))]
        sin5 = [put(f"sin5_{i}", [P, S], at=at_kb(kb)) for i, kb in enumerate((4, 6, 110))]
        bc5 = [put(f"bc5_{i}", [P, 2 * P + 2 * F5], at=at_kb(kb)) for i, kb in enumerate((8, 10))] + [bc5_third]
        c5 = put("c5", [P, 4, 2, F5], at=at_kb(12))
        s5in = put("s5in", [P, 4, S], at=at_kb(16))
        rot = put("rot", [P, 2, 2, S], at=at_kb(24))
        state5 = [put(f"state5_{i}", [P, 2, S], at=at_kb(kb)) for i, kb in enumerate((32, 36, 96, 100))]
        ys_hi = put("ys_hi", [P, 4, S], F32R, at=at_kb(24))
        ys_lo = put("ys_lo", [P, 4, S], F32R, at=at_kb(32))
        yg_hi = put("yg_hi", [P, 4, S], F32R, at=at_kb(40))
        yg_lo = put("yg_lo", [P, 4, S], F32R, at=at_kb(48))
        eq = put("eq", [P, 2, S], at=at_kb(56))
        lt = put("lt", [P, 2, S], at=at_kb(60))
        alow = put("alow", [P, S], at=at_kb(64))
        s_t = put("s_t", [P, 2, 4, P], at=at_kb(66))
        la = put("la", [P, 2, S], at=at_kb(70))
        kend_t = put("kend_t", [P, PAIRS, 2, P], at=at_kb(70))
        ek = put("ek", [P, 2, S], at=at_kb(74))
        q_f = put("q_f", [P, 2, S], at=at_kb(78))
        k_f = put("k_f", [P, 2, S], at=at_kb(82))
        v_t = put("v_t", [P, PAIRS, 4 * DV], at=at_kb(86))
        r_f = put("r_f", [P, 4, S], at=at_kb(94))
        first_of_chunk = put("first_of_chunk", [P, S], at=at_kb(102))
        st = put("st", [P, 2, NCH + 1, DV], at=at_kb(102))
        decay = put("decay", [P, 2, NCH], at=at_kb(111))
        gate = put("gate", [P, 16, S], at=at_kb(56))
        z_f = put("z_f", [P, 4, S], at=at_kb(88))
        z_hi = put("z_hi", [P, 4, S], F32R, at=at_kb(96))
        z_lo = put("z_lo", [P, 4, S], F32R, at=at_kb(104))
        mix_lo_1 = put("mix_lo_1", [P, KD, S], F32R, at=at_kb(40))
        mix_hi_1 = put("mix_hi_1", [P, KD, S], F32R, at=at_kb(96))

        ya_lo = put("ya_lo", [P, HEADS, S], F32R, at=at_kb(0))
        lru_i = put("lru_i", [P, 2, 2, S], at=at_kb(18))
        lru_a = put("lru_a", [P, 2, 2, S], at=at_kb(26))
        lru_v = put("lru_v", [P, 2, 2, S], at=at_kb(34))
        pool_hi = put("pool_hi", [P, KD, S], F32R, at=at_kb(0))
        pool_lo = put("pool_lo", [P, KD, S], F32R, at=at_kb(16))
        win = [put(f"win{i}", [P, S + 2 * EDGE], at=at_kb(34) + 2112 * i) for i in range(3)]
        wg = [diag, put("wg1", [P, 4, P], at=at_kb(42))]
        xa = put("xa", [P, HEADS, S], at=at_kb(44))
        ya_hi = put("ya_hi", [P, HEADS, S], F32R, at=at_kb(44))
        t_hi = put("t_hi", [P, KD, S], F32R, at=at_kb(64))
        t_lo = put("t_lo", [P, KD, S], F32R, at=at_kb(80))
        gate_a = put("gate_a", [P, KD, S], at=at_kb(64))
        gate_b = put("gate_b", [P, KD, S], at=at_kb(96))
        mix_lo_2 = put("mix_lo_2", [P, KD, S], F32R, at=at_kb(20))
        mix_hi_2 = put("mix_hi_2", [P, KD, S], F32R, at=at_kb(80))
        assert at_kb(112) <= 229344, at_kb(112)

        x_kept = nc.dram_tensor("x_kept", [KD, P, S], F32, kind="Internal").ap()
        trig_kept = nc.dram_tensor("trig_kept", [T5, P, 2 * S], F32, kind="Internal").ap()

        bank = [ctx.enter_context(nc.psum_tensor(f"bank{i}", [P, S], F32)) for i in range(8)]
        DB = [bank[0:2], bank[2:4]]
        XB = bank[4:8]

        vec_in = sem("vec_in")
        x_in = [sem(f"x_in{k}") for k in range(KD)]
        const_made = sem("const_made")
        raw_landed = [sem("raw_landed0"), sem("raw_landed1")]
        w_hi = sem("w_hi")
        w_lo = sem("w_lo")
        pe_done = sem("pe_done")
        evac = [sem("evac0"), sem("evac1")]
        act_tile = sem("act_tile")
        gate_in = sem("gate_in")
        h_ready = sem("h_ready")
        acc_ready = sem("acc_ready")
        sums_out = sem("sums_out")
        rt_ready = sem("rt_ready")
        rs_ready = sem("rs_ready")
        diag_ready = sem("diag_ready")
        spread = sem("spread")
        ut_ready = sem("ut_ready")
        uhi_ready = sem("uhi_ready")
        u_ready = sem("u_ready")
        dve_step = sem("dve_step")
        pool_step = sem("pool_step")
        act_step = sem("act_step")
        stored = sem("stored")
        out_ready = sem("out_ready")
        s5_exp = sem("s5_exp")
        s5_angle = sem("s5_angle")
        s5_vecs = sem("s5_vecs")
        turned = sem("turned")
        sines = sem("sines")
        trig_ready = sem("trig_ready")
        trig_out = [sem("trig_out0"), sem("trig_out1")]
        x_done = sem("x_done")
        spilled = sem("spilled")
        x_back = sem("x_back")
        aup_in = sem("aup_in")
        aup_out = sem("aup_out")
        z_neg = sem("z_neg")
        ln_out = sem("ln_out")
        bcum = sem("bcum")
        exps_out = sem("exps_out")
        rest_ready = sem("rest_ready")
        rest_exp = sem("rest_exp")
        gla_in = sem("gla_in")
        kend_out = sem("kend_out")
        kend_in = sem("kend_in")
        scores_out = sem("scores_out")
        masked = sem("masked")
        dstate_out = sem("dstate_out")
        state_in = sem("state_in")
        o_out = sem("o_out")
        o_kept = sem("o_kept")
        yg_ready = sem("yg_ready")
        r_ready = sem("r_ready")
        gate_ready = sem("gate_ready")
        side5_in = [sem(f"side5_in{i}") for i in range(3)]
        bu_out = sem("bu_out")
        bu_read = sem("bu_read")
        scanned = sem("scanned")
        c5_ready = sem("c5_ready")
        re_ready = sem("re_ready")
        im_ready = sem("im_ready")
        y5_out = sem("y5_out")
        z_sum = sem("z_sum")
        z_act = sem("z_act")
        z_ready = sem("z_ready")
        glu_act = sem("glu_act")
        glu_used = sem("glu_used")
        ys_ready = sem("ys_ready")
        lam_exp = sem("lam_exp")
        wg_in = [sem("wg_in0"), sem("wg_in1")]
        xa_ready = sem("xa_ready")
        pooled = sem("pooled")
        t_ready = sem("t_ready")
        lru_out = sem("lru_out")
        lru_gates = sem("lru_gates")
        lru_exp = sem("lru_exp")
        lru_ix = sem("lru_ix")
        lru_var = sem("lru_var")
        lru_root = sem("lru_root")
        lru_product = sem("lru_product")
        lru_scanned = sem("lru_scanned")
        ya_ready = sem("ya_ready")
        wp_out = sem("wp_out")
        wp_read = sem("wp_read")
        gate2_in = sem("gate2_in")
        gate2_ready = sem("gate2_ready")
        mixed = sem("mixed")

        def slot5(j):
            i, k = M1["gs"] + 1, S5_FIRST + int(S5_EVERY * j)
            while k >= (KD if i < M1["pgla"] else 4):
                k -= KD if i < M1["pgla"] else 4
                i += 1
            return i, k

        def pool_banks(nb):
            return XB[0:2], XB[2:4], DB[(nb + M2["wp"][0]) % 2], XB[0:2]

        block = ctx.enter_context(nc.Block())

        @block.sync
        def _(sp):
            def load(nb, it, src, width):
                if not (isinstance(it, int) and nb + 2 * it < 2):
                    sp.wait_ge(w_lo, nb - 1 + 2 * it)
                sp.dma_start(raw[nb % 2][:, 0:width], src).then_inc(raw_landed[nb % 2], 16)

            def ffn(nb, up, down, side=None, first=None):
                m0 = 0
                for h, tiles in enumerate(HALVES):
                    def up_turn(it):
                        for j in range(2):
                            load(nb + j, it, up[m0 + j + 2 * it], UNIT)
                            if first and h == 0 and j == 0 and isinstance(it, int):
                                first()
                        if side and h and isinstance(it, int):
                            side(h - 1, KD // 2 - 1)

                    def down_turn(it):
                        for j in range(2):
                            load(nb + j, it, down[h][j + 2 * it], tiles * P)
                        if side and not isinstance(it, int):
                            side(h, it - 1)
                    rolled(sp, tiles // 2, up_turn, [])
                    nb += tiles
                    rolled(sp, KD // 2, down_turn, [])
                    nb += KD
                    m0 += tiles

            def mixer1(nb):
                src = [A["win1_alow"][0]] + [A["win1"][i] for i in range(16)] \
                    + [A["pgla"][i] for i in range(4)] + [A["glu"][i] for i in range(2)] \
                    + [A["ps5"][i] for i in range(4)] + [A["wout1"][i] for i in range(4)]
                assert len(src) == M1_UNITS

                def side5(j):
                    if j == 0:
                        sp.wait_ge(spilled, 16 * KD)
                        for q in range(2):
                            sp.wait_ge(trig_out[q], 16 * T5 // 2)
                    if j == 2:
                        sp.wait_ge(yg_ready, PAIRS)
                    if j >= 3:
                        sp.wait_ge(re_ready, j - 2)
                        sp.wait_ge(im_ready, j - 2)
                    q = j % 3
                    for dst, src in ((bc5, A["bc5"][j]), (cos5, trig_kept[j, :, 0:S]), (sin5, trig_kept[j, :, S:2 * S])):
                        sp.dma_start(dst[q][:, :], src).then_inc(side5_in[q], 16)

                sent = 0
                for i in range(M1_UNITS):
                    load(nb + i, 0, src[i], src[i].shape[-1])
                    if i == 1:
                        keep_trig(1, KD // 2 - 1)
                        for k in range(KD):
                            if k == 0:
                                sp.wait_ge(x_done, KD)
                            sp.dma_start(x_kept[k], x[:, k, :]).then_inc(spilled, 16)
                    while sent < T5 and i >= M1["gs"] + 1 and (sent < 2 or slot5(sent)[0] <= i - 1):
                        side5(sent)
                        sent += 1
                    if i == M1["wout"] - 1:
                        sp.wait_ge(y5_out, T5)
                        sp.wait_ge(c5_ready, T5)
                        for k in range(KD):
                            sp.dma_start(x[:, k, :], x_kept[k]).then_inc(x_back, 16)
                assert sent == T5

            def mixer2(nb):
                sent = 0
                for i in range(M2_UNITS):
                    name, u = M2_KIND[i]
                    src = A[name + "2"][u]
                    load(nb + i, 0, src, src.shape[-1])
                    if 3 <= i < 7:
                        for k in (2 * (i - 3), 2 * (i - 3) + 1):
                            sp.wait_ge(x_done, KD + k + 1)
                            sp.dma_start(x_kept[k], x[:, k, :]).then_inc(spilled, 16)
                    while sent < HEADS and head_slot(sent)[0] <= i - 1:
                        if sent == 0:
                            sp.wait_ge(spilled, 2 * 16 * KD)
                        if sent >= 2:
                            sp.wait_ge(lru_out, sent - 1)
                        sp.dma_start(wg[sent % 2][:, :, :], A["wg2"][sent]).then_inc(wg_in[sent % 2], 16)
                        sent += 1
                    if i == M2["wout"][1]:
                        sp.wait_ge(pe_done, nb + M2["pa"][-1] + 1)
                        for k in range(KD):
                            sp.dma_start(x[:, k, :], x_kept[k]).then_inc(x_back, 16)

            sp.dma_start(vec[:, :], A["vec"]).then_inc(vec_in, 16)

            def load_x():
                for k in range(KD):
                    sp.dma_start(x[:, k, :], A["xT"][k * P:(k + 1) * P, :]).then_inc(x_in[k], 16)
                sp.dma_start(aup[:, :], A["aup"]).then_inc(aup_in, 16)

            def keep_trig(h, it):
                for j in range(2):
                    sp.wait_ge(trig_ready, KD * h + 2 * it + j + 1)
                    sp.dma_start(trig_kept[KD * h + j + 2 * it], trig[:, j, :]).then_inc(trig_out[j], 16)

            ffn(0, A["up1"], (A["down1a"], A["down1b"]), keep_trig, load_x)
            mixer1(FFN_UNITS)
            nb = FFN_UNITS + M1_UNITS
            ffn(nb, A["up2"], (A["down2a"], A["down2b"]))
            mixer2(nb + FFN_UNITS)
            nb += FFN_UNITS + M2_UNITS
            ffn(nb, A["up3"], (A["down3a"], A["down3b"]))
            for k in range(KD):
                sp.wait_ge(out_ready, k + 1)
                sp.dma_start(out[k * P:(k + 1) * P, :], x[:, k, :]).then_inc(stored, 16)
            sp.wait_ge(stored, 16 * KD)

        @block.gpsimd
        def _(pool):
            def low(nb, it, width):
                pool.wait_ge(w_hi, nb + 1 + 2 * it)
                s = nb % 2
                pool.tensor_tensor(out=wlo[s][:, 0:width], in0=raw[s][:, 0:width],
                                   in1=whi[s][:, 0:width].bitcast(F32), op=ALU.subtract).then_inc(w_lo, 1)

            steps = Tally(pool_step)

            def then(ins):
                ins.then_inc(pool_step, 1)
                pool.wait_ge(pool_step, steps.step())

            norms = Tally(rt_ready)

            def inverse_root(width=4):
                pool.wait_ge(rt_ready, norms.step())
                pool.tensor_tensor(out=nstat[:, 0:width], in0=nstat[:, 0:width], in1=nstat[:, 8:8 + width],
                                   op=ALU.pow).then_inc(rs_ready, 1)

            def ffn(nb, first=None):
                for h, tiles in enumerate(HALVES):
                    def up_turn(it):
                        for j in range(2):
                            low(nb + j, it, UNIT)
                            if h == 0 and j == 1 and isinstance(it, int) and first:
                                first()

                    def down_turn(it):
                        for j in range(2):
                            low(nb + j, it, tiles * P)
                    rolled(pool, tiles // 2, up_turn, [])
                    nb += tiles
                    rolled(pool, KD // 2, down_turn, [])
                    nb += KD

            def mixer1(nb):
                widths = [D] + 16 * [UNIT] + 10 * [4 * 2 * P] + 4 * [UNIT]

                def imaginary(j):
                    q = j % 2
                    pool.wait_ge(side5_in[j % 3], 48 * (j // 3 + 1))
                    pool.wait_ge(scanned, 2 * (j + 1))
                    pool.tensor_tensor(out=ut[:, 0, :], in0=rot[:, q, 0, :], in1=sin5[j % 3][:, :], op=ALU.mult)
                    then(pool.tensor_tensor(out=ut[:, 1, :], in0=rot[:, q, 1, :], in1=cos5[j % 3][:, :], op=ALU.mult))
                    if j >= 4:
                        pool.wait_ge(y5_out, j - 3)
                    pool.tensor_tensor(out=state5[j % 4][:, 1, :], in0=ut[:, 0, :], in1=ut[:, 1, :], op=ALU.add)\
                        .then_inc(im_ready, 1)
                    pool.wait_ge(im_ready, j + 1)

                done5 = 0
                for i in range(M1_UNITS):
                    low(nb + i, 0, widths[i])
                    if i == 0:
                        inverse_root()
                    if M1["r"] + 2 <= i < M1["r"] + 2 + PAIRS:
                        inverse_root()
                    while done5 < T5 and slot5(done5)[0] <= i - 1:
                        if done5 == 0:
                            pool.wait_ge(yg_ready, PAIRS)
                        imaginary(done5)
                        done5 += 1
                assert done5 == T5

            pool.iota(steps5[:, :], pattern=[[1, S]], base=0, channel_multiplier=0,
                      allow_small_or_imprecise_dtypes=True)
            pool.memset(half_pi, float(np.pi / 2))
            for n, w in enumerate(WINDOWS):
                last = pool.memset(per_count[:, n, :], 1.0 / w)
            then(last)
            for n, w in enumerate(WINDOWS):
                for e in range(w // 2):
                    pool.memset(per_count[:, n, e:e + 1], 1.0 / (e + w // 2))
                for e in range(1, w // 2):
                    pool.memset(per_count[:, n, 2 * EDGE - e:2 * EDGE - e + 1], 1.0 / (e + w // 2))
            then(pool.memset(causal[:, :], 1.0))
            then(pool.affine_select(out=causal[:, :], in_=causal[:, :], compare_op=ALU.is_ge, fill=0.0, base=0,
                                    pattern=[[1, P]], channel_multiplier=-1))
            pool.memset(causal[0:CHUNK, CHUNK:P], 0.0)
            pool.memset(ones[:, :], 1.0)
            pool.memset(nstat[:, 8:16], -0.5)
            then(pool.memset(ident[:, :], 0.0))
            pool.affine_select(out=ident[:, :], in_=ident[:, :], compare_op=ALU.not_equal, fill=1.0, base=0,
                               pattern=[[-1, P]], channel_multiplier=1).then_inc(const_made, 1)
            pool.wait_ge(const_made, 1)
            ffn(0, inverse_root)
            mixer1(FFN_UNITS)
            nb = FFN_UNITS + M1_UNITS
            ffn(nb, inverse_root)
            nb += FFN_UNITS
            for i in range(M2_UNITS):
                low(nb + i, 0, A[M2_KIND[i][0] + "2"].shape[-1])
                if i == 1:
                    inverse_root(8)
                for h in range(HEADS):
                    if head_turn(h) == i:
                        q = h % 2
                        pool.wait_ge(lru_gates, h + 1)
                        pool.tensor_tensor(out=lru_i[:, q, :, :], in0=lru_i[:, q, :, :],
                                           in1=xa[:, h:h + 1, :].broadcast_to([P, 2, S]), op=ALU.mult)\
                            .then_inc(lru_ix, 1)
            nb += M2_UNITS
            ffn(nb, inverse_root)
            inverse_root()

        @block.scalar
        def _(act):
            def high(nb, it, width):
                s = nb % 2
                act.wait_ge(raw_landed[s], 16 * (nb // 2 + 1) + 16 * it)
                if not (isinstance(it, int) and nb + 2 * it < 2):
                    act.wait_ge(pe_done, nb - 1 + 2 * it)
                act.activation(whi[s][:, 0:width], raw[s][:, 0:width], ACT.Copy).then_inc(w_hi, 1)

            steps = Tally(act_step)
            turns = Tally(turned)

            def then(ins):
                ins.then_inc(act_step, 1)
                act.wait_ge(act_step, steps.step())

            def small5():
                lams = vec[:, VECS["lam_f_2"]:VECS["lam_f_2"] + 2 * HEADS]
                then(act.activation(lam[:, 2, :], lams, ACT.Abs))
                act.activation(lam[:, 2, :], lam[:, 2, :], ACT.Exp, scale=-1.0).then_inc(lam_exp, 1)
                act.activation(v5[:, 0, :], vec[:, VECS["log_dt"]:VECS["log_dt"] + T5], ACT.Exp).then_inc(s5_exp, 1)
                act.wait_ge(s5_angle, 1)
                act.activation(v5[:, 1, :], v5[:, 1, :], ACT.Exp)
                then(act.activation(v5[:, 4, :], v5[:, 3, :], ACT.Abs))
                act.activation(v5[:, 5, :], v5[:, 3, :], ACT.Sin, scale=0.5)
                act.activation(v5[:, 6, :], v5[:, 4, :], ACT.Sin, scale=-0.5, bias=half_pi).then_inc(s5_exp, 1)

            def trig_tiles():
                for j in range(2):
                    act.wait_ge(turned, turns.step())
                    act.activation(turn_s[:, j, :], turn[:, j, :], ACT.Sin, scale=float(np.pi))
                    then(act.activation(turn_c[:, j, :], turn[:, j, :], ACT.Abs))
                    act.activation(turn_c[:, j, :], turn_c[:, j, :], ACT.Sin, scale=-float(np.pi), bias=half_pi)
                    act.activation(turn_q[:, j, :], turn_s[:, j, :], ACT.Square, scale=float(np.sqrt(2.0)))\
                        .then_inc(sines, 1)

            def mixer1(nb):
                widths = [D] + 16 * [UNIT] + 10 * [4 * 2 * P] + 4 * [UNIT]

                def bank_of(i, m):
                    return DB[(nb + i) % 2][m][:, :]

                def log_gate():
                    for m in range(2):
                        act.wait_ge(z_neg, m + 1)
                        b = VECS["gla_a_up_b"] + m
                        last = act.activation(lt[:, m, :], XB[m][:, :], ACT.Abs, bias=vec[:, b:b + 1])
                    then(last)
                    then(act.activation(lt[:, :, :], lt[:, :, :], ACT.Exp, scale=-1.0))
                    act.activation(lt[:, :, :], lt[:, :, :], ACT.Ln, bias=ones[:, 0:1]).then_inc(ln_out, 1)

                def decays():
                    act.wait_ge(bcum, 2)
                    act.activation(eq[:, :, :], la[:, :, :], ACT.Exp, scale=1.0 / 16)
                    act.activation(ek[:, :, :], la[:, :, :], ACT.Exp, scale=-1.0 / 16).then_inc(exps_out, 1)

                def decay_rest():
                    act.wait_ge(rest_ready, 1)
                    act.activation(lt[:, :, :], lt[:, :, :], ACT.Exp, scale=1.0 / 16).then_inc(rest_exp, 1)

                def keep_kend():
                    act.wait_ge(kend_out, 1)
                    for half in range(2):
                        act.activation(kend_t[:, 2 * half:2 * half + 2, :, :], XB[half][:, :], ACT.Copy)\
                            .then_inc(kend_in, 1)

                def keep_o(p):
                    act.wait_ge(o_out, p + 1)
                    if p:
                        act.wait_ge(yg_ready, p)
                    act.activation(ut[:, 0, :], XB[3][:, :], ACT.Copy)
                    act.activation(ut[:, 1, :], XB[3][:, :], ACT.Square).then_inc(o_kept, 1)

                def silu_r(u):
                    i = M1["r"] + u
                    act.wait_ge(pe_done, nb + i + 1)
                    act.activation(r_f[:, 2 * u, :], bank_of(i, 0), ACT.Silu).then_inc(r_ready, 1)
                    act.activation(r_f[:, 2 * u + 1, :], bank_of(i, 1), ACT.Silu).then_inc(evac[(nb + i) % 2], 1)
                    act.wait_ge(evac[(nb + i) % 2], (nb + i) // 2 + 1)
                    act.nop().then_inc(r_ready, 1)

                def sigmoids(u):
                    i = M1["gs"] + u
                    act.wait_ge(pe_done, nb + i + 1)
                    if u == 1:
                        act.wait_ge(yg_ready, PAIRS)
                    act.activation(gate[:, 2 * u, :], bank_of(i, 0), ACT.Sigmoid).then_inc(gate_ready, 1)
                    act.activation(gate[:, 2 * u + 1, :], bank_of(i, 1), ACT.Sigmoid).then_inc(evac[(nb + i) % 2], 1)

                def gelu_z(m):
                    act.wait_ge(z_sum, m + 1)
                    act.activation(z_f[:, m, :], z_f[:, m, :], ACT.Gelu_apprx_tanh).then_inc(z_act, 1)

                def glu(u):
                    i = M1["glu"] + u
                    act.wait_ge(pe_done, nb + i + 1)
                    for m in range(2):
                        if u:
                            act.wait_ge(glu_used, m + 1)
                        b = VECS["s5_glu_b"] + 2 * u + m
                        a = act.activation(ut[:, m, :], bank_of(i, m), ACT.Sigmoid, bias=vec[:, b:b + 1])
                        a.then_inc(glu_act, 1)

                jobs = {1: [norm_high], 2: [log_gate], 3: [decays], 4: [decay_rest],
                        6: [keep_kend, lambda: silu_r(0)], 7: [lambda: keep_o(0), lambda: silu_r(1)],
                        8: [lambda: keep_o(1)], 9: [lambda: keep_o(2)], 10: [lambda: keep_o(3)]}
                for u in range(8):
                    jobs.setdefault(M1["gs"] + u + 1, []).append(lambda u=u: sigmoids(u))
                for m, i in enumerate((13, 15, 17, 20)):
                    jobs.setdefault(i, []).insert(0, lambda m=m: gelu_z(m))
                for u in range(2):
                    jobs.setdefault(M1["glu"] + u + 1, []).append(lambda u=u: glu(u))
                for i in range(M1_UNITS):
                    high(nb + i, 0, widths[i])
                    for job in jobs.get(i, ()):
                        job()

            def mixer2(nb):
                def gates(name, u):
                    dst, b, at = (gate_a, 0, 4) if name == "ga" else (gate_b, 8, 0)
                    act.wait_ge(gate2_in, at + u + 1)
                    for m in range(2):
                        c = VECS["b_gate_2"] + b + 2 * u + m
                        last = act.activation(dst[:, 2 * u + m, :], dst[:, 2 * u + m, :], ACT.Sigmoid,
                                              bias=vec[:, c:c + 1])
                    last.then_inc(gate2_ready, 1)

                def lru_functions(h):
                    q = h % 2
                    if h >= 2:
                        act.wait_ge(lru_product, h - 1)
                    if h:
                        act.wait_ge(lru_exp, 2 * h)
                    act.wait_ge(lru_out, h + 1)
                    for d in range(2):
                        for n, (name, dst) in enumerate((("ba", ut[:, d, :]), ("bx", lru_i[:, q, d, :]))):
                            c = VECS[name + "_" + "fb"[d] + "_2"] + h
                            last = act.activation(dst, XB[2 * d + n][:, :], ACT.Sigmoid, bias=vec[:, c:c + 1])
                    last.then_inc(lru_gates, 1)
                    act.wait_ge(lru_gates, h + 1)
                    if h >= 2:
                        act.wait_ge(lru_scanned, h - 1)
                    for d in range(2):
                        c = d * HEADS + h
                        act.activation(lru_v[:, q, d, :], ut[:, d, :], ACT.Tanh, scale=lam[:, 0, c:c + 1])
                    if h:
                        lru_roots(h - 1)
                    for d in range(2):
                        c = d * HEADS + h
                        act.activation(lru_a[:, q, d, :], ut[:, d, :], ACT.Exp, scale=lam[:, 1, c:c + 1])\
                            .then_inc(lru_exp, 1)

                def lru_roots(h):
                    q = h % 2
                    act.wait_ge(lru_var, h + 1)
                    act.activation(lru_v[:, q, :, :], lru_v[:, q, :, :], ACT.Sqrt).then_inc(lru_root, 1)

                for i in range(M2_UNITS):
                    high(nb + i, 0, A[M2_KIND[i][0] + "2"].shape[-1])
                    for h in range(HEADS):
                        if head_turn(h) == i:
                            lru_functions(h)
                            if h == HEADS - 1:
                                lru_roots(h)
                    if i >= 2 and M2_KIND[i - 2][0] in ("ga", "gb"):
                        gates(*M2_KIND[i - 2])

            tiles_u = Tally(ut_ready)

            def norm_high():
                for k in range(KD):
                    act.wait_ge(ut_ready, tiles_u.step())
                    act.activation(uhi[:, k, :], ut[:, k % 2, :], ACT.Copy).then_inc(uhi_ready, 1)

            gates_in = Tally(gate_in)

            def gate_tile(nb, func):
                s = nb % 2
                act.wait_ge(gate_in, gates_in.step())
                act.activation(sil[:, s, :], cva[:, s, :], func).then_inc(act_tile, 1)

            def ffn(nb, func, first=None, side=None):
                for h, tiles in enumerate(HALVES):
                    def up_turn(it):
                        alone = isinstance(it, int)
                        for j in range(2):
                            high(nb + j, it, UNIT)
                            if not (alone and it == 0):
                                gate_tile(nb + j, func)

                    def down_turn(it):
                        for j in range(2):
                            high(nb + j, it, tiles * P)
                            if isinstance(it, int) and it == 0:
                                gate_tile(nb - 2 + j, func)
                        if side:
                            side()
                    up_turn(0)
                    if first and h == 0:
                        up_turn(1)
                        first()
                        rolled_on(act, 2, tiles // 2, up_turn, [gates_in])
                    else:
                        rolled_on(act, 1, tiles // 2, up_turn, [gates_in])
                    nb += tiles
                    rolled(act, KD // 2, down_turn, [turns, steps])
                    nb += KD

            act.wait_ge(vec_in, 16)
            act.wait_ge(const_made, 1)

            ffn(0, ACT.Silu, small5, trig_tiles)
            mixer1(FFN_UNITS)
            nb = FFN_UNITS + M1_UNITS
            ffn(nb, ACT.Silu)
            mixer2(nb + FFN_UNITS)
            nb += FFN_UNITS + M2_UNITS
            ffn(nb, ACT.Gelu_apprx_tanh)

        @block.tensor
        def _(pe):
            def product(dst, w, cols, hi, lo, first, last):
                wh, wl = w[0][:, cols], w[1][:, cols]
                pe.matmul(dst, wh, hi, start=first, stop=False)
                pe.matmul(dst, wh, lo, start=False, stop=False)
                return pe.matmul(dst, wl, hi, start=False, stop=last)

            def unit(nb, it, K, M, hi, lo, ready=None, between={}):
                s = nb % 2
                pe.wait_ge(w_lo, nb + 1 + 2 * it)
                if not (isinstance(it, int) and nb + 2 * it < 2):
                    pe.wait_ge(evac[s], nb // 2 + it)
                for k in range(K):
                    for job in between.get(k, ()):
                        job()
                    if ready:
                        ready(k)
                    for m in range(M):
                        at = (k * M + m) * P
                        last = product(DB[s][m][:, :], (whi[s], wlo[s]), slice(at, at + P),
                                       hi[:, k, :], lo[:, k, :], k == 0, k == K - 1)
                last.then_inc(pe_done, 1)

            nacc = Tally(acc_ready)
            ndiag = Tally(diag_ready)

            def sum_squares(accs=(acc,)):
                pe.wait_ge(acc_ready, nacc.step())
                for n, a in enumerate(accs):
                    for c in range(4):
                        last = pe.matmul(XB[0][:, 4 * n + c:4 * n + c + 1], a[:, c * P:(c + 1) * P],
                                         ones[:, 0:1], start=True, stop=True)
                last.then_inc(sums_out, 1)

            def spread_roots(to=1):
                pe.wait_ge(diag_ready, ndiag.step())
                for c in range(4):
                    last = pe.matmul(XB[to][:, c * P:(c + 1) * P], ones[:, :], diag[:, c, :],
                                     start=True, stop=True)
                last.then_inc(spread, 1)

            rooted = {7: [sum_squares]}, {3: [spread_roots]}
            rooted_first = {}, {1: [sum_squares], 5: [spread_roots]}

            us = [0]

            def u_tile(k):
                pe.wait_ge(u_ready, us[0] + k + 1)

            hs = [0]

            def ffn(nb, rooted=rooted):
                for h, tiles in enumerate(HALVES):
                    def up_turn(it):
                        alone = isinstance(it, int)
                        for j in range(2):
                            unit(nb + j, it, KD, 2, uhi, ulo,
                                 u_tile if alone and j == 0 and h == 0 else None,
                                 rooted[j] if alone and h == 0 else {})

                    def down_turn(it):
                        alone = isinstance(it, int)
                        for j in range(2):
                            unit(nb + j, it, tiles, 1, hhi, hlo,
                                 (lambda k: pe.wait_ge(h_ready, hs[0] + k + 1)) if alone and j == 0 else None)
                    rolled(pe, tiles // 2, up_turn, [])
                    nb += tiles
                    rolled(pe, KD // 2, down_turn, [])
                    nb += KD
                    hs[0] += tiles
                us[0] += KD

            def mixer1(nb):
                def a_up():
                    pe.wait_ge(aup_in, 16)
                    pe.wait_ge(evac[nb % 2], nb // 2 + 1)
                    for m in range(2):
                        last = pe.matmul(XB[m][:, :], aup[:, m * P:(m + 1) * P], alow[:, :], start=True, stop=True)
                    last.then_inc(aup_out, 1)

                def v_unit(i):
                    s = (nb + i) % 2
                    pe.wait_ge(w_lo, nb + i + 1)
                    pe.wait_ge(evac[s], (nb + i) // 2)
                    for t in range(PAIRS):
                        dst = DB[s][t // 2][:, (t % 2) * 2 * P:(t % 2 + 1) * 2 * P]
                        tok = slice(t * P, (t + 1) * P)
                        for k in range(KD):
                            cols = slice(k * 2 * P, (k + 1) * 2 * P)
                            pe.matmul(dst, uhi[:, k, tok], whi[s][:, cols], start=k == 0, stop=False)
                            pe.matmul(dst, uhi[:, k, tok], wlo[s][:, cols], start=False, stop=False)
                            last = pe.matmul(dst, ulo[:, k, tok], whi[s][:, cols], start=False, stop=k == KD - 1)
                    last.then_inc(pe_done, 1)

                def turn_kend():
                    pe.wait_ge(gla_in, 1)
                    for p in range(PAIRS):
                        for g in range(2):
                            at = ((p % 2) * 2 + g) * P
                            last = pe.transpose(XB[p // 2][:, at:at + P], k_f[:, g, p * P:(p + 1) * P], ident[:, :])
                    last.then_inc(kend_out, 1)

                def head(h):
                    return h // 2, slice(DK * (h % 2), DK * (h % 2) + DK)

                def q_of(h):
                    return eq if h % 2 else q_f

                def scores(p):
                    pe.wait_ge(gla_in, 1)
                    if p:
                        pe.wait_ge(masked, p)
                    tok = slice(p * P, (p + 1) * P)
                    for h in range(4):
                        g, rows = head(h)
                        last = pe.matmul(XB[2][:, h * P:(h + 1) * P], ek[:, g, tok], q_of(h)[:, g, tok],
                                         start=True, stop=True)
                    last.then_inc(scores_out, 1)

                def state_steps(p):
                    pe.wait_ge(kend_in, 2)
                    if p:
                        pe.wait_ge(yg_ready, p)
                    for c in range(2):
                        rows_t = slice(c * CHUNK, (c + 1) * CHUNK)
                        for h in range(4):
                            g, rows = head(h)
                            last = pe.matmul(XB[c][rows, g * P:(g + 1) * P],
                                             kend_t[rows_t, p, g, rows], v_t[rows_t, p, h * DV:(h + 1) * DV],
                                             start=True, stop=True)
                    last.then_inc(dstate_out, 1)

                def outputs(p):
                    pe.wait_ge(masked, p + 1)
                    pe.wait_ge(state_in, p + 1)
                    if p:
                        pe.wait_ge(o_kept, p)
                    for h in range(4):
                        g, rows = head(h)
                        pe.matmul(XB[3][:, h * P:(h + 1) * P], v_t[:, p, h * DV:(h + 1) * DV],
                                  s_t[:, p % 2, h, :], start=True, stop=False)
                        for c in range(2):
                            at = h * P + c * CHUNK
                            tok = slice(p * P + c * CHUNK, p * P + (c + 1) * CHUNK)
                            last = pe.matmul(XB[3][:, at:at + CHUNK], st[:, g, 2 * p + c, :],
                                             q_of(h)[:, g, tok], start=False, stop=c == 1)
                    last.then_inc(o_out, 1)

                def o_sums(p):
                    pe.wait_ge(o_kept, p + 1)
                    for h in range(4):
                        last = pe.matmul(XB[0][:, h:h + 1], ut[:, 1, h * P:(h + 1) * P], ones[:, 0:1],
                                         start=True, stop=True)
                    last.then_inc(sums_out, 1)

                def o_spread(p):
                    pe.wait_ge(diag_ready, ndiag.step())
                    for h in range(4):
                        last = pe.matmul(XB[1][:, h * P:(h + 1) * P], ones[:, :], diag[:, h, :], start=True, stop=True)
                    last.then_inc(spread, 1)

                def drive(j):
                    pe.wait_ge(side5_in[j % 3], 48 * (j // 3 + 1))
                    if j == 0:
                        s = (nb + M1["s5"] + 1) % 2
                        pe.wait_ge(evac[s], (nb + M1["s5"] + 1) // 2 + 1)
                        pe.wait_ge(yg_ready, PAIRS)
                    else:
                        pe.wait_ge(bu_read, j)
                    for c in range(2):
                        last = pe.matmul(XB[c][:, :], bc5[j % 3][:, c * P:(c + 1) * P], s5in[:, j // 4, :],
                                         start=True, stop=True)
                    last.then_inc(bu_out, 1)

                def read_out(j):
                    m = j // 4
                    for n in (j, j + 1):
                        pe.wait_ge(re_ready, n + 1)
                        pe.wait_ge(im_ready, n + 1)
                        pe.wait_ge(c5_ready, n + 1)
                    if j % 4 == 0 and m >= 2:
                        pe.wait_ge(z_sum, m - 1)
                    for part in range(2):
                        for n in (j, j + 1):
                            rows = slice(F5 * (n % 4), F5 * (n % 4 + 1))
                            last = pe.matmul(XB[2 + m % 2][rows, :], c5[:, n % 4, part, :], state5[n % 4][:, part, :],
                                             start=part == 0, stop=part == 1)
                    last.then_inc(y5_out, 2)

                gla_slots = (0, scores), (4, state_steps), (6, outputs), (7, o_sums), (9, o_spread)
                between = {i: {} for i in range(M1_UNITS)}
                between[1][4] = [a_up]
                between[5][2] = [turn_kend]
                for p in range(PAIRS):
                    for k, job in gla_slots:
                        between[6 + p + k // KD].setdefault(k % KD, []).append(lambda job=job, p=p: job(p))
                for j in range(T5 + 2):
                    i, k = slot5(j)
                    here = between[i].setdefault(k, [])
                    if j < T5:
                        here.append(lambda j=j: drive(j))
                    if j >= 3 and j % 2:
                        here.append(lambda j=j: read_out(j - 3))

                sum_squares()
                spread_roots()
                for i in range(M1_UNITS):
                    if M1["v"] <= i < M1["v"] + 2:
                        v_unit(i)
                    elif i < M1["pgla"]:
                        unit(nb + i, 0, KD, 1 if i == 0 else 2, uhi, ulo, u_tile if i == 0 else None, between[i])
                    elif i < M1["glu"]:
                        unit(nb + i, 0, 4, 2, yg_hi, yg_lo, None, between[i])
                    elif i < M1["ps5"]:
                        unit(nb + i, 0, 4, 2, z_hi, z_lo, (lambda k: pe.wait_ge(z_ready, k + 1)))
                    elif i < M1["wout"]:
                        unit(nb + i, 0, 4, 2, ys_hi, ys_lo, (lambda k: pe.wait_ge(ys_ready, k + 1)))
                    else:
                        unit(nb + i, 0, KD, 2, mix_hi_1, mix_lo_1, lambda k: pe.wait_ge(mixed, k + 1))
                    if i == 0:
                        us[0] += KD

            pe.wait_ge(const_made, 1)
            def mixer2(nb):
                def head_gates(h):
                    q = h % 2
                    pe.wait_ge(wg_in[q], 16 * (h // 2 + 1))
                    pe.wait_ge(xa_ready, HEADS)
                    if h:
                        pe.wait_ge(lru_gates, h)
                    else:
                        pe.wait_ge(wp_read, 3)
                    for n in range(4):
                        last = pe.matmul(XB[n][:, :], wg[q][:, n, :], xa[:, h, :],
                                         start=True, stop=True)
                    last.then_inc(lru_out, 1)

                def pool_unit(i):
                    s = (nb + i) % 2
                    pe.wait_ge(w_lo, nb + i + 1)
                    pe.wait_ge(evac[s], (nb + i) // 2)
                    for g in range(4):
                        if g == 3:
                            pe.wait_ge(wp_read, 1)
                        for k in range(2):
                            pe.wait_ge(pooled, 2 * g + k + 1)
                            for m in range(2):
                                at = ((2 * g + k) * 2 + m) * P
                                last = product(pool_banks(nb)[g][m][:, :], (whi[s], wlo[s]), slice(at, at + P),
                                               pool_hi[:, 2 * g + k, :], pool_lo[:, 2 * g + k, :], k == 0, k == 1)
                        last.then_inc(wp_out if g < 3 else pe_done, 1)

                between = {i: {} for i in range(M2_UNITS)}
                between[0] = {5: [lambda: sum_squares((acc, acc_2))]}
                between[1] = {1: [spread_roots], 5: [lambda: spread_roots(2)]}
                for h in range(HEADS):
                    i, k = head_slot(h)
                    between[i].setdefault(k, []).append(lambda h=h: head_gates(h))
                for i in range(M2_UNITS):
                    name, u = M2_KIND[i]
                    side = between[i]
                    if name in ("ua", "ub", "ga", "gb"):
                        unit(nb + i, 0, KD, 2, uhi, ulo, u_tile if i == 0 else None, side)
                    elif name == "wp":
                        pool_unit(i)
                    elif name == "pb":
                        unit(nb + i, 0, KD, 2, t_hi, t_lo, lambda k: pe.wait_ge(t_ready, k + 1), side)
                    elif name == "pa":
                        unit(nb + i, 0, HEADS, 1, ya_hi, ya_lo, lambda k: pe.wait_ge(ya_ready, k + 1))
                    else:
                        unit(nb + i, 0, KD, 2, mix_hi_2, mix_lo_2, lambda k: pe.wait_ge(mixed, KD + k + 1))
                us[0] += KD

            ffn(0, rooted_first)
            mixer1(FFN_UNITS)
            nb = FFN_UNITS + M1_UNITS
            ffn(nb)
            mixer2(nb + FFN_UNITS)
            nb += FFN_UNITS + M2_UNITS
            ffn(nb)
            sum_squares()
            spread_roots()

        @block.vector
        def _(dve):
            steps = Tally(dve_step)

            def then(ins):
                ins.then_inc(dve_step, 1)
                dve.wait_ge(dve_step, steps.step())

            def col(name, k=0):
                c = VECS[name] + k
                return vec[:, c:c + 1]

            def square_in(k):
                then(dve.tensor_tensor(out=sq[:, :], in0=x[:, k, :], in1=x[:, k, :], op=ALU.mult))
                then(dve.tensor_tensor(out=acc[:, :], in0=acc[:, :], in1=sq[:, :], op=ALU.add))

            n_norm = Tally(sums_out)
            n_rs = Tally(rs_ready)
            n_spread = Tally(spread)

            def means(sums, over):
                dve.wait_ge(sums_out, n_norm.step())
                dve.tensor_scalar(nstat[:, 0:4], sums, 1.0 / over, EPS, ALU.mult, ALU.add).then_inc(rt_ready, 1)
                dve.wait_ge(rs_ready, n_rs.step())

            def root():
                dve.engine_nop().then_inc(acc_ready, 1)
                means(XB[0][:, 0:4], D)
                diagonals(0)
                dve.wait_ge(spread, n_spread.step())

            def diagonals(at):
                for c in range(4):
                    last = dve.tensor_scalar(diag[:, c, :], ident[:, :], nstat[:, at + c:at + c + 1], None, ALU.mult)
                last.then_inc(diag_ready, 1)

            def prepare(gain, m):
                g = gain(m)
                then(dve.tensor_scalar(uhi[:, m, :], x[:, m, :], g, None, ALU.mult))
                dve.scalar_tensor_tensor(out=ulo[:, m, :], in0=x[:, m, :], scalar=g, in1=uhi[:, m, :].bitcast(F32),
                                         op0=ALU.mult, op1=ALU.subtract).then_inc(u_ready, 1)

            def gain_of(name):
                return lambda m: vec[:, bass.ds(VECS[name] + m, 1)]

            def keep_inverse(inv):
                then(dve.tensor_copy(inv[:, :], XB[1][:, :]))

            n_uhi = Tally(uhi_ready)
            n_u = [0]

            def norm(gain):
                root()

                def lower(k):
                    dve.wait_ge(uhi_ready, n_uhi.step())
                    dve.tensor_tensor(out=ulo[:, k, :], in0=ut[:, k % 2, :], in1=uhi[:, k, :].bitcast(F32),
                                      op=ALU.subtract).then_inc(u_ready, 1)
                    n_u[0] += 1
                for k in range(KD):
                    if k >= 2:
                        dve.wait_ge(u_ready, n_u[0])
                    dve.scalar_tensor_tensor(out=ut[:, k % 2, :], in0=x[:, k, :], scalar=col(gain, k),
                                             in1=XB[1][:, :], op0=ALU.mult, op1=ALU.mult).then_inc(ut_ready, 1)
                    if k >= 1:
                        lower(k - 1)
                lower(KD - 1)

            def norm_x(gain, ready, bank):
                for k in range(KD):
                    dve.scalar_tensor_tensor(out=x[:, k, :], in0=x[:, k, :], scalar=col(gain, k),
                                             in1=bank[:, :], op0=ALU.mult, op1=ALU.mult).then_inc(ready, 1)

            gates = Tally(act_tile)
            n_h = Tally(h_ready)

            def split_h(src, m):
                then(dve.tensor_copy(hhi[:, m, :], src))
                dve.tensor_tensor(out=hlo[:, m, :], in0=src, in1=hhi[:, m, :].bitcast(F32),
                                  op=ALU.subtract).then_inc(h_ready, 1)

            def up_tile(nb, it, m, inv):
                s = nb % 2
                dve.wait_ge(pe_done, nb + 1 + 2 * it)
                dve.tensor_tensor(out=cva[:, s, :], in0=DB[s][0][:, :], in1=inv[:, :], op=ALU.mult)\
                   .then_inc(gate_in, 1)
                dve.tensor_tensor(out=cvb[:, s, :], in0=DB[s][1][:, :], in1=inv[:, :], op=ALU.mult)\
                   .then_inc(evac[s], 1)
                dve.wait_ge(evac[s], nb // 2 + 1 + it)
                dve.wait_ge(act_tile, gates.step())
                then(dve.tensor_tensor(out=ht[:, s, :], in0=cvb[:, s, :], in1=sil[:, s, :], op=ALU.mult))

            n_sines = Tally(sines)
            n_out = [Tally(trig_out[0]), Tally(trig_out[1])]

            def turns_of(h, it):
                for j in range(2):
                    tile = KD * h + 2 * it + j
                    hi, lo = v5[:, 12, bass.ds(tile, 1)], v5[:, 13, bass.ds(tile, 1)]
                    then(dve.tensor_scalar(turn_t[:, j, :], steps5[:, :], hi, ROUND, ALU.mult, ALU.add))
                    then(dve.tensor_scalar(turn_t[:, j, :], turn_t[:, j, :], ROUND, None, ALU.subtract))
                    then(dve.scalar_tensor_tensor(out=turn_t[:, j, :], in0=steps5[:, :], scalar=hi,
                                                  in1=turn_t[:, j, :], op0=ALU.mult, op1=ALU.subtract))
                    dve.scalar_tensor_tensor(out=turn[:, j, :], in0=steps5[:, :], scalar=lo, in1=turn_t[:, j, :],
                                             op0=ALU.mult, op1=ALU.add).then_inc(turned, 1)

            def trig_from(it):
                for j in range(2):
                    dve.wait_ge(sines, n_sines.step())
                    if not isinstance(it, int) or trig_slot_used[0]:
                        dve.wait_ge(trig_out[j], n_out[j].step(16))
                    dve.tensor_scalar(trig[:, j, 0:S], turn_q[:, j, :], -1.0, 1.0, ALU.mult, ALU.add)
                    dve.scalar_tensor_tensor(out=trig[:, j, S:2 * S], in0=turn_s[:, j, :], scalar=2.0,
                                             in1=turn_c[:, j, :], op0=ALU.mult, op1=ALU.mult).then_inc(trig_ready, 1)

            trig_slot_used = [False]

            def conv_tile(nb, it, m, inv):
                s = nb % 2
                dve.wait_ge(pe_done, nb + 1 + 2 * it)
                dve.tensor_tensor(out=conv_src[:, 0, :], in0=DB[s][0][:, :], in1=inv[:, :], op=ALU.mult)
                dve.tensor_tensor(out=conv_src[:, 1, :], in0=DB[s][1][:, :], in1=inv[:, :], op=ALU.mult)\
                   .then_inc(evac[s], 1)
                dve.wait_ge(evac[s], nb // 2 + 1 + it)
                for half, dst in ((0, cva), (1, cvb)):
                    src = conv_src[:, half, :]
                    tap = [vec[:, bass.ds(VECS["conv_f_w_2"] + 44 * k + 22 * half + m, 1)] for k in range(3)]
                    bias = vec[:, bass.ds(VECS["conv_f_b_2"] + 22 * half + m, 1)]
                    then(dve.tensor_scalar(dst[:, s, :], src, tap[1], bias, ALU.mult, ALU.add))
                    then(dve.scalar_tensor_tensor(out=dst[:, s, 1:S], in0=src[:, 0:S - 1], scalar=tap[0],
                                                  in1=dst[:, s, 1:S], op0=ALU.mult, op1=ALU.add))
                    ins = dve.scalar_tensor_tensor(out=dst[:, s, 0:S - 1], in0=src[:, 1:S], scalar=tap[2],
                                                   in1=dst[:, s, 0:S - 1], op0=ALU.mult, op1=ALU.add)
                    if half:
                        then(ins)
                    else:
                        ins.then_inc(gate_in, 1)
                dve.wait_ge(act_tile, gates.step())
                then(dve.tensor_tensor(out=ht[:, s, :], in0=cvb[:, s, :], in1=sil[:, s, :], op=ALU.mult))

            def ffn(nb, tile, inv, trig_of=False, share=0.5, then_gain=None, twice=False):
                for h, tiles in enumerate(HALVES):
                    def up_turn(it):
                        for j in range(2):
                            tile(nb + j, it, 2 * it + j + sum(HALVES[:h]), inv)
                            split_h(ht[:, (nb + j) % 2, :], 2 * it + j)

                    def down_turn(it, ahead=trig_of):
                        for j in range(2):
                            if trig_of and j:
                                trig_from(it)
                                if ahead:
                                    turns_of(h, it + 1)
                            s, m = (nb + j) % 2, 2 * it + j
                            dve.wait_ge(pe_done, nb + j + 1 + 2 * it)
                            dve.scalar_tensor_tensor(out=x[:, m, :], in0=DB[s][0][:, :], scalar=share,
                                                     in1=x[:, m, :], op0=ALU.mult, op1=ALU.add).then_inc(evac[s], 1)
                            if h == 1:
                                dve.wait_ge(evac[s], (nb + j) // 2 + 1 + it)
                                square_in(m)
                                if twice:
                                    then(dve.scalar_tensor_tensor(out=sq[:, :], in0=x[:, m, :],
                                                                  scalar=gains[:, 0, bass.ds(m, 1)],
                                                                  in1=x[:, m, :], op0=ALU.mult, op1=ALU.mult))
                                    then(dve.tensor_tensor(out=acc_2[:, :], in0=acc_2[:, :], in1=sq[:, :],
                                                           op=ALU.add))
                                if then_gain:
                                    prepare(then_gain, m)
                    if trig_of and h == 0:
                        up_turn(0)
                        small5()
                        turns_of(0, 0)
                        rolled_on(dve, 1, tiles // 2, up_turn, [gates, steps])
                    else:
                        rolled(dve, tiles // 2, up_turn, [gates, steps])
                    nb += tiles
                    if h == 1:
                        if twice:
                            dve.memset(acc_2[:, :], 0.0)
                        then(dve.memset(acc[:, :], 0.0))
                    if trig_of and h == 0:
                        down_turn(0)
                        trig_slot_used[0] = True
                        rolled_on(dve, 1, KD // 2, down_turn, [steps, n_sines, n_out[0], n_out[1]])
                    elif trig_of:
                        small_lru()
                        rolled_on(dve, 0, KD // 2 - 1, down_turn, [steps, n_sines, n_out[0], n_out[1]])
                        down_turn(KD // 2 - 1, False)
                    else:
                        rolled(dve, KD // 2, down_turn, [steps, n_sines, n_out[0], n_out[1]])
                    nb += KD
                if then_gain:
                    n_u[0] += KD

            LRE, LIM, DT = (vec[:, VECS[n]:VECS[n] + T5] for n in ("lam_re", "lam_im", "log_dt"))

            def small5():
                tt, ts, stt = dve.tensor_tensor, dve.tensor_scalar, dve.scalar_tensor_tensor

                def v(i):
                    return v5[:, i, :]
                dve.wait_ge(s5_exp, 1)
                then(tt(out=v(1), in0=LRE, in1=v(0), op=ALU.mult))
                then(tt(out=v(3), in0=LIM, in1=v(0), op=ALU.mult))
                then(ts(v(2), v(3), 1.0 / TAU, ROUND, ALU.mult, ALU.add))
                then(ts(v(2), v(2), ROUND, None, ALU.subtract))
                for part in (TAU_1, TAU_2, TAU_3):
                    then(stt(out=v(3), in0=v(2), scalar=-part, in1=v(3), op0=ALU.mult, op1=ALU.add))
                dve.engine_nop().then_inc(s5_angle, 1)
                dve.wait_ge(s5_exp, 2)
                then(tt(out=v(7), in0=v(5), in1=v(5), op=ALU.mult))
                then(ts(v(7), v(7), -2.0, 1.0, ALU.mult, ALU.add))
                then(stt(out=v(8), in0=v(5), scalar=2.0, in1=v(6), op0=ALU.mult, op1=ALU.mult))
                then(tt(out=v(7), in0=v(7), in1=v(1), op=ALU.mult))
                then(tt(out=v(8), in0=v(8), in1=v(1), op=ALU.mult))
                then(ts(v(7), v(7), 1.0, None, ALU.subtract))
                then(tt(out=v(10), in0=LRE, in1=LRE, op=ALU.mult))
                then(tt(out=v(11), in0=LIM, in1=LIM, op=ALU.mult))
                then(tt(out=v(10), in0=v(10), in1=v(11), op=ALU.add))
                then(dve.reciprocal(v(10), v(10)))
                then(tt(out=v(11), in0=v(7), in1=LRE, op=ALU.mult))
                then(tt(out=v(12), in0=v(8), in1=LIM, op=ALU.mult))
                then(tt(out=v(11), in0=v(11), in1=v(12), op=ALU.add))
                then(tt(out=v(12), in0=v(8), in1=LRE, op=ALU.mult))
                then(tt(out=v(13), in0=v(7), in1=LIM, op=ALU.mult))
                then(tt(out=v(12), in0=v(12), in1=v(13), op=ALU.subtract))
                then(tt(out=v(7), in0=v(11), in1=v(10), op=ALU.mult))
                then(tt(out=v(8), in0=v(12), in1=v(10), op=ALU.mult))
                then(ts(v(9), v(8), -1.0, None, ALU.mult))
                then(ts(v(11), v(3), 1.0 / TAU, None, ALU.mult))
                then(ts(v(12), v(11), ROUND13, ROUND13, ALU.add, ALU.subtract))
                then(tt(out=v(13), in0=v(11), in1=v(12), op=ALU.subtract))

            def small_lru():
                tt, ts, stt = dve.tensor_tensor, dve.tensor_scalar, dve.scalar_tensor_tensor

                def v(i):
                    return lam[:, i, :]
                lams = vec[:, VECS["lam_f_2"]:VECS["lam_f_2"] + 2 * HEADS]
                dve.wait_ge(lam_exp, 1)
                then(ts(v(3), v(2), 2.0, None, ALU.add))
                then(dve.reciprocal(v(3), v(3)))
                then(tt(out=v(2), in0=v(2), in1=v(3), op=ALU.mult))
                then(tt(out=v(3), in0=v(2), in1=v(2), op=ALU.mult))
                then(ts(v(4), v(3), 1.0 / 15, 1.0 / 13, ALU.mult, ALU.add))
                for n in (11, 9, 7, 5, 3, 1):
                    then(tt(out=v(4), in0=v(4), in1=v(3), op=ALU.mult))
                    then(ts(v(4), v(4), 1.0 / n, None, ALU.add))
                then(stt(out=v(4), in0=v(4), scalar=2.0, in1=v(2), op0=ALU.mult, op1=ALU.mult))
                then(ts(v(3), lams, -1.0, 0.0, ALU.mult, ALU.max))
                then(tt(out=v(4), in0=v(4), in1=v(3), op=ALU.add))
                ts(v(0), v(4), LRU_C, None, ALU.mult)
                then(ts(v(1), v(4), -LRU_C, None, ALU.mult))

            def mixer2(nb):
                tt, ts, stt = dve.tensor_tensor, dve.tensor_scalar, dve.scalar_tensor_tensor

                def bank_of(i, m):
                    return DB[(nb + i) % 2][m][:, :]

                def done(i):
                    dve.wait_ge(pe_done, nb + i + 1)

                def freed(i, ins):
                    s = (nb + i) % 2
                    ins.then_inc(evac[s], 1)
                    dve.wait_ge(evac[s], (nb + i) // 2 + 1)

                def split(hi, lo, src, ready):
                    then(dve.tensor_copy(hi, src))
                    tt(out=lo, in0=src, in1=hi.bitcast(F32), op=ALU.subtract).then_inc(ready, 1)

                def conv_in(u):
                    i = M2["ua"][u]
                    done(i)
                    for m in range(2):
                        ins = tt(out=ut[:, m, :], in0=bank_of(i, m), in1=inv_late[:, :], op=ALU.mult)
                    freed(i, ins)
                    for m in range(2):
                        n = 2 * u + m
                        src, dst = ut[:, m, :], xa[:, n, :]
                        tap = [col("conv_a_w_2", HEADS * k + n) for k in range(4)]
                        then(ts(dst, src, tap[2], col("conv_a_b_2", n), ALU.mult, ALU.add))
                        for k, off in ((0, 2), (1, 1)):
                            then(stt(out=dst[:, off:S], in0=src[:, 0:S - off], scalar=tap[k], in1=dst[:, off:S],
                                     op0=ALU.mult, op1=ALU.add))
                        stt(out=dst[:, 0:S - 1], in0=src[:, 1:S], scalar=tap[3], in1=dst[:, 0:S - 1],
                            op0=ALU.mult, op1=ALU.add).then_inc(xa_ready, 1)
                    dve.wait_ge(xa_ready, 2 * (u + 1))

                def windows(g):
                    i = M2["ub"][g]
                    done(i)
                    for m in range(2):
                        ins = tt(out=win[0][:, EDGE:EDGE + S], in0=bank_of(i, m), in1=inv_late[:, :], op=ALU.mult)
                        if m:
                            freed(i, ins)
                        else:
                            then(ins)
                        src, end = win[0], S + 2 * EDGE
                        then(tt(out=win[1][:, 1:end], in0=src[:, 0:end - 1], in1=src[:, 1:end], op=ALU.add))
                        have, lost, now, other = 2, 1, win[1], win[2]
                        while have < WINDOWS[g]:
                            d = have // 2
                            then(tt(out=other[:, lost + d:end - d], in0=now[:, lost:end - 2 * d],
                                    in1=now[:, lost + 2 * d:end], op=ALU.add))
                            have, lost, end, now, other = 2 * have, lost + d, end - d, other, now
                        mean = other[:, 0:S]
                        sums, tok = now[:, EDGE:EDGE + S], src[:, EDGE:EDGE + S]
                        then(stt(out=mean, in0=sums, scalar=1.0 / WINDOWS[g], in1=tok, op0=ALU.mult,
                                 op1=ALU.subtract))
                        for side, at in ((0, 0), (1, S - EDGE)):
                            part = mean[:, at:at + EDGE]
                            then(tt(out=part, in0=sums[:, at:at + EDGE],
                                    in1=per_count[:, g, side * EDGE:(side + 1) * EDGE], op=ALU.mult))
                            then(tt(out=part, in0=part, in1=tok[:, at:at + EDGE], op=ALU.subtract))
                        split(pool_hi[:, 2 * g + m, :], pool_lo[:, 2 * g + m, :], mean, pooled)
                        dve.wait_ge(pooled, 2 * g + m + 1)

                def pool_out(g):
                    if g < 3:
                        dve.wait_ge(wp_out, g + 1)
                    else:
                        done(M2["wp"][0])
                    for m in range(2):
                        n = 2 * g + m
                        ins = ts(sq[:, :], pool_banks(nb)[g][m][:, :], col("b_pool_2", n), col("pool_scale_2", n),
                                 ALU.add, ALU.mult)
                        if m and g == 2:
                            freed(M2["wp"][0], ins)
                        elif m:
                            ins.then_inc(wp_read, 1)
                            dve.wait_ge(wp_read, min(g + 1, 3))
                        else:
                            then(ins)
                        split(t_hi[:, n, :], t_lo[:, n, :], sq[:, :], t_ready)
                        dve.wait_ge(t_ready, n + 1)

                def gate_inputs(name, u):
                    i = M2[name][u]
                    dst = gate_a if name == "ga" else gate_b
                    done(i)
                    tt(out=dst[:, 2 * u, :], in0=bank_of(i, 0), in1=inv_late[:, :], op=ALU.mult)
                    freed(i, tt(out=dst[:, 2 * u + 1, :], in0=bank_of(i, 1), in1=inv_late[:, :], op=ALU.mult))
                    dve.engine_nop().then_inc(gate2_in, 1)

                def pool_branch(u):
                    i = M2["pb"][u]
                    done(i)
                    dve.wait_ge(gate2_ready, u + 1)
                    for m in range(2):
                        last = tt(out=gate_b[:, 2 * u + m, :], in0=bank_of(i, m), in1=gate_b[:, 2 * u + m, :],
                                  op=ALU.mult)
                    freed(i, last)

                def lru_variance(h):
                    q = h % 2
                    v = lru_v[:, q, :, :]
                    dve.wait_ge(lru_exp, 2 * (h + 1))
                    then(tt(out=squares[:, :, :], in0=lru_a[:, q, :, :], in1=lru_a[:, q, :, :], op=ALU.mult))
                    stt(out=v, in0=squares[:, :, :], scalar=1.0, in1=v, op0=ALU.add, op1=ALU.mult)\
                        .then_inc(lru_var, 1)

                def lru_scans(h):
                    q = h % 2
                    v = lru_v[:, q, :, :]
                    dve.wait_ge(lru_ix, h + 1)
                    dve.wait_ge(lru_root, h + 1)
                    tt(out=v, in0=v, in1=lru_i[:, q, :, :], op=ALU.mult).then_inc(lru_product, 1)
                    dve.wait_ge(lru_product, h + 1)
                    for d, way in ((0, slice(None)), (1, slice(None, None, -1))):
                        last = dve.tensor_tensor_scan(squares[:, d, way], lru_a[:, q, d, way], lru_v[:, q, d, way],
                                                      0.0, ALU.mult, ALU.add)
                    last.then_inc(lru_scanned, 1)
                    dve.wait_ge(lru_scanned, h + 1)
                    then(tt(out=acc[:, :], in0=squares[:, 0, :], in1=squares[:, 1, :], op=ALU.add))
                    split(ya_hi[:, h, :], ya_lo[:, h, :], acc[:, :], ya_ready)
                    dve.wait_ge(ya_ready, h + 1)

                def merge(u):
                    i = M2["pa"][u]
                    done(i)
                    dve.wait_ge(gate2_ready, 4 + u // 2 + 1)
                    freed(i, tt(out=sq[:, :], in0=bank_of(i, 0), in1=gate_a[:, u, :], op=ALU.mult))
                    then(tt(out=sq[:, :], in0=sq[:, :], in1=gate_b[:, u, :], op=ALU.add))
                    split(mix_hi_2[:, u, :], mix_lo_2[:, u, :], sq[:, :], mixed)
                    dve.wait_ge(mixed, KD + u + 1)

                def residual(u):
                    i = M2["wout"][u]
                    done(i)
                    for n in range(2):
                        m = 2 * u + n
                        ins = tt(out=x[:, m, :], in0=bank_of(i, n), in1=x[:, m, :], op=ALU.add)
                    freed(i, ins)
                    for n in range(2):
                        square_in(2 * u + n)
                        prepare(gain_of("g_ffn_2"), 2 * u + n)

                def two_roots():
                    dve.engine_nop().then_inc(acc_ready, 1)
                    dve.wait_ge(sums_out, n_norm.step())
                    ts(nstat[:, 4:8], XB[0][:, 4:8], 1.0 / D, None, ALU.mult)
                    then(ts(nstat[:, 0:4], XB[0][:, 0:4], 1.0 / D, EPS, ALU.mult, ALU.add))
                    then(dve.reciprocal(sq[:, 0:4], nstat[:, 0:4]))
                    then(tt(out=nstat[:, 4:8], in0=nstat[:, 4:8], in1=sq[:, 0:4], op=ALU.mult))
                    ts(nstat[:, 4:8], nstat[:, 4:8], EPS, None, ALU.add).then_inc(rt_ready, 1)
                    dve.wait_ge(rs_ready, n_rs.step())
                    then(tt(out=nstat[:, 4:8], in0=nstat[:, 0:4], in1=nstat[:, 4:8], op=ALU.mult))
                    diagonals(4)
                    dve.wait_ge(spread, n_spread.step())
                    keep_inverse(inv_late)
                    diagonals(0)

                two_roots()
                conv_in(0)
                dve.wait_ge(spread, n_spread.step())
                norm_x("final_norm", x_done, XB[2])
                for u in range(1, len(M2["ua"])):
                    conv_in(u)
                for w in win:
                    last = dve.memset(w[:, :], 0.0)
                then(last)
                dve.wait_ge(spilled, 2 * 16 * KD)
                for g in range(4):
                    windows(g)
                gate_inputs("gb", 0)
                gate_inputs("gb", 1)
                for g in range(4):
                    pool_out(g)
                units = list(range(M2["wp"][0] + 1, M2["pa"][0]))

                def side_units(until):
                    while units and KD * (units[0] - M2["wp"][0]) <= until:
                        name, u = M2_KIND[units.pop(0)]
                        if name == "pb":
                            pool_branch(u)
                        else:
                            gate_inputs(name, u)
                for h in range(HEADS):
                    side_units(HEAD_FIRST + int(HEAD_EVERY * h))
                    lru_variance(h)
                    side_units(HEAD_FIRST + int(HEAD_EVERY * (h + 1)) + SIDE_LATE)
                    lru_scans(h)
                side_units(KD * M2_UNITS)
                for u in range(KD):
                    merge(u)
                then(dve.memset(acc[:, :], 0.0))
                dve.wait_ge(x_back, 2 * 16 * KD)
                for u in range(4):
                    residual(u)

            def mixer1(nb):
                tt, ts, stt = dve.tensor_tensor, dve.tensor_scalar, dve.scalar_tensor_tensor

                def bank_of(i, m):
                    return DB[(nb + i) % 2][m][:, :]

                def done(i):
                    dve.wait_ge(pe_done, nb + i + 1)

                def freed(i, ins):
                    s = (nb + i) % 2
                    ins.then_inc(evac[s], 1)
                    dve.wait_ge(evac[s], (nb + i) // 2 + 1)

                def copy_out(i, dst, scale=None):
                    done(i)
                    for m in range(2):
                        last = ts(dst[:, m, :], bank_of(i, m), scale, None, ALU.mult) if scale else \
                            dve.tensor_copy(dst[:, m, :], bank_of(i, m))
                    freed(i, last)

                def values(u):
                    i = M1["v"] + u
                    done(i)
                    for half in range(2):
                        last = dve.tensor_copy(v_t[:, 2 * half:2 * half + 2, u * 2 * P:(u + 1) * 2 * P],
                                               bank_of(i, half).rearrange("p (t n) -> p t n", t=2))
                    freed(i, last)

                def gated_r(u):
                    dve.wait_ge(r_ready, 2 * (u + 1))
                    for m in (2 * u, 2 * u + 1):
                        last = ts(r_f[:, m, :], r_f[:, m, :], col("gla_out_norm", m), None, ALU.mult)
                    then(last)

                def mask(p):
                    dve.wait_ge(scores_out, p + 1)
                    then(dve.memset(s_t[:, p % 2, :, :], 0.0))
                    dve.copy_predicated(s_t[:, p % 2, :, :], causal[:, :].bitcast(U32).unsqueeze(1)
                                        .broadcast_to([P, 4, P]), XB[2][:, :].rearrange("p (h q) -> p h q", h=4))\
                       .then_inc(masked, 1)

                def states(p):
                    dve.wait_ge(dstate_out, p + 1)
                    for c in range(2):
                        n = 2 * p + c
                        for g in range(2):
                            last = stt(out=st[:, g, n + 1, :], in0=st[:, g, n, :], scalar=decay[:, g, n:n + 1],
                                       in1=XB[c][:, g * P:(g + 1) * P],
                                       op0=ALU.mult, op1=ALU.add)
                        if c == 0:
                            then(last)
                    last.then_inc(state_in, 1)
                    dve.wait_ge(state_in, p + 1)
                    means(XB[0][:, 0:4], DV)
                    diagonals(0)

                def pair_out(p):
                    dve.wait_ge(spread, n_spread.step())
                    tok = slice(p * P, (p + 1) * P)
                    then(tt(out=sq[:, :], in0=ut[:, 0, :], in1=XB[1][:, :], op=ALU.mult))
                    y = sq[:, :].rearrange("p (h q) -> p h q", h=4)
                    then(tt(out=y, in0=y, in1=r_f[:, :, tok], op=ALU.mult))
                    then(dve.tensor_copy(yg_hi[:, :, tok], y))
                    tt(out=yg_lo[:, :, tok], in0=y, in1=yg_hi[:, :, tok].bitcast(F32), op=ALU.subtract)\
                        .then_inc(yg_ready, 1)
                    dve.wait_ge(yg_ready, p + 1)

                def state_tile(j):
                    q = j % 2
                    cos, sin = cos5[j % 3][:, :], sin5[j % 3][:, :]
                    wr, wi = rot[:, q, 0, :], rot[:, q, 1, :]
                    dve.wait_ge(side5_in[j % 3], 48 * (j // 3 + 1))
                    dve.wait_ge(bu_out, j + 1)
                    if j >= 2:
                        dve.wait_ge(im_ready, j - 1)
                    tt(out=wr, in0=XB[0][:, :], in1=cos, op=ALU.mult)
                    tt(out=sq[:, :], in0=XB[1][:, :], in1=sin, op=ALU.mult)
                    tt(out=wi, in0=XB[1][:, :], in1=cos, op=ALU.mult)
                    tt(out=acc[:, :], in0=XB[0][:, :], in1=sin, op=ALU.mult).then_inc(bu_read, 1)
                    dve.wait_ge(bu_read, j + 1)
                    tt(out=wr, in0=wr, in1=sq[:, :], op=ALU.add)
                    then(tt(out=wi, in0=wi, in1=acc[:, :], op=ALU.subtract))
                    mag = v5[:, 1, j:j + 1].broadcast_to([P, S])
                    for w in (wr, wi):
                        dve.tensor_tensor_scan(w, mag, w, 0.0, ALU.mult, ALU.add).then_inc(scanned, 1)
                    if j >= 4:
                        dve.wait_ge(y5_out, j - 3)
                    fr, fi, nfi = (v5[:, i, j:j + 1] for i in (7, 8, 9))
                    cr, ci = bc5[j % 3][:, 2 * P:2 * P + F5], bc5[j % 3][:, 2 * P + F5:2 * P + 2 * F5]
                    re, im = c5[:, j % 4, 0, :], c5[:, j % 4, 1, :]
                    ts(re, ci, fi, None, ALU.mult)
                    then(ts(im, ci, fr, None, ALU.mult))
                    stt(out=re, in0=cr, scalar=fr, in1=re, op0=ALU.mult, op1=ALU.subtract)
                    stt(out=im, in0=cr, scalar=nfi, in1=im, op0=ALU.mult, op1=ALU.subtract).then_inc(c5_ready, 1)
                    dve.wait_ge(scanned, 2 * (j + 1))
                    tt(out=sq[:, :], in0=wr, in1=cos, op=ALU.mult)
                    then(tt(out=acc[:, :], in0=wi, in1=sin, op=ALU.mult))
                    tt(out=state5[j % 4][:, 0, :], in0=sq[:, :], in1=acc[:, :], op=ALU.subtract).then_inc(re_ready, 1)
                    dve.wait_ge(re_ready, j + 1)

                def z_in(m):
                    dve.wait_ge(y5_out, 4 * (m + 1))
                    stt(out=z_f[:, m, :], in0=s5in[:, m, :], scalar=col("s5_d", m), in1=XB[2 + m % 2][:, :],
                        op0=ALU.mult, op1=ALU.add).then_inc(z_sum, 1)

                def z_split(m):
                    dve.wait_ge(z_act, m + 1)
                    then(dve.tensor_copy(z_hi[:, m, :], z_f[:, m, :]))
                    tt(out=z_lo[:, m, :], in0=z_f[:, m, :], in1=z_hi[:, m, :].bitcast(F32), op=ALU.subtract)\
                        .then_inc(z_ready, 1)

                def attention_branch(u):
                    i = M1["pgla"] + u
                    done(i)
                    for m in range(2):
                        g = gate[:, 8 + 2 * u + m, :]
                        last = tt(out=g, in0=bank_of(i, m), in1=g, op=ALU.mult)
                    freed(i, last)

                def glu(u):
                    i = M1["glu"] + u
                    for m in range(2):
                        n = 2 * u + m
                        dve.wait_ge(glu_act, n + 1)
                        tt(out=sq[:, :], in0=z_f[:, n, :], in1=ut[:, m, :], op=ALU.mult).then_inc(glu_used, 1)
                        dve.wait_ge(glu_used, n + 1)
                        then(dve.tensor_copy(ys_hi[:, n, :], sq[:, :]))
                        last = tt(out=ys_lo[:, n, :], in0=sq[:, :], in1=ys_hi[:, n, :].bitcast(F32), op=ALU.subtract)
                        last.then_inc(ys_ready, 1)
                        dve.wait_ge(ys_ready, n + 1)
                    dve.engine_nop().then_inc(evac[(nb + i) % 2], 1)

                def merge(i, m, a, b):
                    done(i)
                    for n in range(2):
                        ins = tt(out=sq[:, :], in0=bank_of(i, n), in1=a[:, m + n, :], op=ALU.mult)
                        if n:
                            freed(i, ins)
                        else:
                            then(ins)
                        then(tt(out=sq[:, :], in0=sq[:, :], in1=b[:, m + n, :], op=ALU.add))
                        then(dve.tensor_copy(mix_hi_1[:, m + n, :], sq[:, :]))
                        tt(out=mix_lo_1[:, m + n, :], in0=sq[:, :], in1=mix_hi_1[:, m + n, :].bitcast(F32),
                           op=ALU.subtract).then_inc(mixed, 1)
                        dve.wait_ge(mixed, m + n + 1)

                def residual(i, m):
                    done(i)
                    for n in range(2):
                        ins = tt(out=x[:, m + n, :], in0=bank_of(i, n), in1=x[:, m + n, :], op=ALU.add)
                    freed(i, ins)
                    for n in range(2):
                        square_in(m + n)
                        prepare(gain_of("ffn2_norm"), m + n)

                norm("mix_norm")
                done(0)
                freed(0, dve.tensor_copy(alow[:, :], bank_of(0, 0)))
                for q in range(2):
                    dve.wait_ge(trig_out[q], 16 * T5 // 2)
                then(dve.memset(first_of_chunk[:, :], 1.0))
                then(dve.memset(first_of_chunk[:, ::CHUNK], 0.0))
                dve.wait_ge(aup_out, 1)
                for m in range(2):
                    ts(la[:, m, :], XB[m][:, :], col("gla_a_up_b", m), 0.0, ALU.add, ALU.min).then_inc(z_neg, 1)
                copy_out(M1["k"], k_f)
                dve.wait_ge(ln_out, 1)
                then(tt(out=la[:, :, :], in0=la[:, :, :], in1=lt[:, :, :], op=ALU.subtract))
                for m in range(2):
                    dve.tensor_tensor_scan(la[:, m, :], first_of_chunk[:, :], la[:, m, :], 0.0, ALU.mult, ALU.add)\
                       .then_inc(bcum, 1)
                copy_out(M1["q"], q_f, DK ** -0.5)
                dve.wait_ge(exps_out, 1)
                la4 = la[:, :, :].rearrange("p m (n c) -> p m n c", c=CHUNK)
                for m in range(2):
                    last = tt(out=lt[:, m, :].rearrange("p (n c) -> p n c", c=CHUNK),
                              in0=la4[:, m, :, CHUNK - 1:CHUNK].broadcast_to([P, NCH, CHUNK]),
                              in1=la4[:, m, :, :], op=ALU.subtract)
                last.then_inc(rest_ready, 1)
                dve.tensor_copy(decay[:, :, :], eq[:, :, CHUNK - 1::CHUNK])
                then(tt(out=ek[:, :, :], in0=k_f[:, :, :], in1=ek[:, :, :], op=ALU.mult))
                then(tt(out=eq[:, :, :], in0=q_f[:, :, :], in1=eq[:, :, :], op=ALU.mult))
                dve.memset(q_f[DK:P, :, :], 0.0)
                then(dve.tensor_copy(q_f[0:DK, :, :], eq[0:DK, :, :]))
                dve.memset(eq[0:DK, :, :], 0.0)
                dve.memset(st[:, :, 0, :], 0.0)
                dve.wait_ge(rest_exp, 1)
                tt(out=k_f[:, :, :], in0=k_f[:, :, :], in1=lt[:, :, :], op=ALU.mult).then_inc(gla_in, 1)
                values(0)
                values(1)
                gated_r(0)
                for p in range(PAIRS):
                    mask(p)
                    if p == 1:
                        gated_r(1)
                        dve.wait_ge(spilled, 16 * KD)
                    if p:
                        pair_out(p - 1)
                    if p >= 2:
                        copy_out(M1["s5"] + p - 2, s5in[:, 2 * (p - 2):2 * (p - 1), :])
                    states(p)
                pair_out(PAIRS - 1)
                for j in range(T5):
                    state_tile(j)
                    if j in (5, 9, 13):
                        z_in(j // 4 - 1)
                attention_branch(0)
                z_in(3)
                z_split(0)
                z_split(1)
                attention_branch(1)
                z_split(2)
                z_split(3)
                attention_branch(2)
                attention_branch(3)
                glu(0)
                glu(1)
                for u in range(4):
                    merge(M1["ps5"] + u, 2 * u, gate, gate[:, 8:16, :])
                then(dve.memset(acc[:, :], 0.0))
                dve.wait_ge(x_back, 16 * KD)
                for u in range(4):
                    residual(M1["wout"] + u, 2 * u)

            then(dve.memset(acc[:, :], 0.0))
            dve.wait_ge(vec_in, 16)
            for k in range(KD):
                dve.wait_ge(x_in[k], 16)
                square_in(k)
                prepare(gain_of("ffn1_norm"), k)
            n_u[0] += KD
            dve.wait_ge(const_made, 1)
            root()
            keep_inverse(inv_first)
            ffn(0, up_tile, inv_first, True)
            dve.engine_nop().then_inc(x_done, KD)
            mixer1(FFN_UNITS)
            n_u[0] += KD
            nb = FFN_UNITS + M1_UNITS
            root()
            keep_inverse(inv_late)
            tt = dve.tensor_tensor
            final, g2 = (vec[:, VECS[n]:VECS[n] + KD] for n in ("final_norm", "g_mix_2"))
            tt(out=gains[:, 0, :], in0=final, in1=final, op=ALU.mult)
            then(tt(out=gains[:, 1, :], in0=final, in1=g2, op=ALU.mult))
            ffn(nb, up_tile, inv_late, then_gain=lambda m: gains[:, 1, bass.ds(m, 1)], twice=True)
            mixer2(nb + FFN_UNITS)
            nb += FFN_UNITS + M2_UNITS
            root()
            keep_inverse(inv_late)
            ffn(nb, conv_tile, inv_late, share=1.0)
            root()
            norm_x("g_final_2", out_ready, XB[1])


def tiles(w, m):
    k, n = w.shape
    return np.ascontiguousarray(w.reshape(k // P, P, n // (m * P), m * P).transpose(2, 1, 0, 3)
                                ).reshape(n // (m * P), P, -1)


def up_units(a, b):
    w = np.stack([a, b]).reshape(2, KD, P, FF // P, P)
    return np.ascontiguousarray(w.transpose(3, 2, 1, 0, 4)).reshape(FF // P, P, UNIT)


def b_and_c(g):
    out = np.zeros((T5, P, 2 * P + 2 * F5), np.float32)
    for j in range(T5):
        for q in range(2):
            grp = 2 * j + q
            f = slice(32 * (j % 4) + H5 * q, 32 * (j % 4) + H5 * (q + 1))
            n = slice(P5 * q, P5 * (q + 1))
            for i, name in enumerate(("s5_b_re", "s5_b_im")):
                out[j, f, P * i + P5 * q:P * i + P5 * (q + 1)] = g[name][0, grp].T
            for i, name in enumerate(("s5_c_re", "s5_c_im")):
                at = 2 * P + F5 * i + H5 * q
                out[j, n, at:at + H5] = g[name][0, grp].T
    return out


def by_feature(v):
    return np.asarray(v, dtype=v.dtype).reshape(-1, P).T


def lay_out(inp):
    g = {k: np.asarray(v) for k, v in inp.items()}
    a = {}
    a["xT"] = np.ascontiguousarray(g["x"][0].T)
    v = np.zeros((P, N_VECS), np.float32)

    def vput(name, cols):
        v[:, VECS[name]:VECS[name] + cols.shape[1]] = cols
    for name in ("ffn1_norm", "mix_norm", "ffn2_norm", "final_norm", "g_mix_2", "g_ffn_2", "g_final_2",
                 "gla_a_up_b", "gla_out_norm", "s5_d", "s5_glu_b", "b_gate_2", "conv_a_w_2", "conv_a_b_2",
                 "ba_f_2", "bx_f_2", "lam_f_2", "ba_b_2", "bx_b_2", "lam_b_2", "b_pool_2", "pool_scale_2",
                 "conv_f_w_2", "conv_f_b_2"):
        vput(name, by_feature(g[name]))
    vput("lam_re", by_feature(g["s5_lambda_re"]))
    vput("lam_im", by_feature(g["s5_lambda_im"]))
    vput("log_dt", by_feature(np.repeat(g["s5_log_dt"].reshape(-1), 64)))
    a["vec"] = v
    cut = HALVES[0] * P
    up2 = g["w_up_2"][0]
    for n, (w1, w3, w2) in {"1": (g["ffn1_w1"][0], g["ffn1_w3"][0], "ffn1_w2"),
                            "2": (g["ffn2_w1"][0], g["ffn2_w3"][0], "ffn2_w2"),
                            "3": (up2[:, :FF], up2[:, FF:], "w_down_2")}.items():
        a["up" + n] = up_units(w1, w3)
        a[f"down{n}a"] = tiles(g[w2][0][:cut], 1)
        a[f"down{n}b"] = tiles(g[w2][0][cut:], 1)
    w = g["w_in"][0]
    at = np.cumsum([0, 512, 256, 256, 512, 512, 16, D, D])
    s5, q, k, v_, r, low, gs, gg = (w[:, at[i]:at[i + 1]] for i in range(8))
    a["win1"] = tiles(np.concatenate([k, q, v_, r, s5, gs, gg], 1), 2)
    a["win1_alow"] = tiles(np.pad(low, ((0, 0), (0, P - 16))), 1)
    a["aup"] = np.pad(g["gla_a_up_w"][0], ((0, P - 16), (0, 0)))
    a["bc5"] = b_and_c(g)
    a["glu"] = tiles(g["s5_glu_w"][0], 2)
    a["ps5"] = tiles(g["proj_s5"][0], 2)
    a["pgla"] = tiles(g["proj_gla"][0], 2)
    a["wout1"] = tiles(g["w_out"][0], 2)
    w = g["w_in_2"][0]
    ua, ub, ga, gb = (w[:, i:j] for i, j in ((0, 1280), (1280, 2304), (2304, 3328), (3328, 4352)))
    a["ua2"], a["ub2"], a["ga2"], a["gb2"] = (tiles(t, 2) for t in (ua, ub, ga, gb))
    a["wp2"] = np.ascontiguousarray(g["w_pool_2"][0].reshape(4, 2, P, 2 * P).transpose(2, 0, 1, 3)).reshape(1, P, -1)
    a["pb2"] = tiles(g["p_b_2"][0], 2)
    a["pa2"] = tiles(g["p_a_2"][0], 1)
    a["wout2"] = tiles(g["w_out_2"][0], 2)
    a["wg2"] = np.ascontiguousarray(np.stack([g[n][0] for n in ("wa_f_2", "wx_f_2", "wa_b_2", "wx_b_2")])
                                    .transpose(1, 2, 0, 3)).reshape(HEADS, P, 4 * P)
    return a


def kernel(**inputs):
    import concourse.bacc as bacc
    from concourse.bass_utils import run_bass_kernel_spmd

    nc = bacc.Bacc("TRN2", target_bir_lowering=False, num_devices=1)
    arrays = {"in_" + k: v for k, v in lay_out(inputs).items()}
    aps = {k[3:]: nc.dram_tensor(k, v.shape, mybir.dt.from_np(v.dtype), kind="ExternalInput").ap()
           for k, v in arrays.items()}
    out = nc.dram_tensor("out_xT", (D, S), F32, kind="ExternalOutput").ap()
    build(nc, aps, out)
    r = run_bass_kernel_spmd(nc, [arrays], core_ids=[0])
    return np.ascontiguousarray(r.results[0]["out_xT"].T)[None]
```
